# Optimizing a Trainium2 kernel written in Bass

```python
import jax, jax.numpy as jnp
from jax import lax
import numpy as np
import math
import jax
import jax.numpy as jnp

D_MODEL = 1024
BATCH = 1
SEQ = 512
DEPTH = 2

BLOCK = 128
NORM_EPS = 1e-6
SWA_WINDOW = 128
SWA_HEADS = 4
SWA_KV_HEADS = 2
SWA_HEAD_DIM = 64
CONV_WIDTH = 256
CONV_K = 3
MLA_HEADS = 4
MLA_Q_RANK = 256
MLA_KV_RANK = 128
MLA_NOPE_DIM = 64
MLA_ROPE_DIM = 32
MLA_V_DIM = 64
ROPE_THETA = 10000.0
SB_HEADS = 4
SB_HEAD_DIM = 64
GROUP_WIDTH = 256
N_GROUPS = 4
D_MIX = GROUP_WIDTH * N_GROUPS

A_Q = SWA_HEADS * SWA_HEAD_DIM
A_KV = SWA_KV_HEADS * SWA_HEAD_DIM
SB_W = SB_HEADS * SB_HEAD_DIM
IN_SIZES = (A_Q, A_KV, A_KV,
            CONV_WIDTH, CONV_WIDTH, CONV_WIDTH,
            MLA_Q_RANK, MLA_KV_RANK, MLA_ROPE_DIM,
            SB_W, SB_W, SB_W,
            D_MIX)
D_IN = int(sum(IN_SIZES))
SPLIT_IDX = [int(v) for v in np.cumsum(IN_SIZES)[:-1]]


def rmsnorm(x, g):
    x32 = x.astype(jnp.float32)
    y = x32 * lax.rsqrt(jnp.mean(x32 * x32, axis=-1, keepdims=True) + NORM_EPS)
    return (y * g.astype(jnp.float32)).astype(x.dtype)

def to_blocks(t):
    b, s = t.shape[:2]
    t = t.reshape((b, s // BLOCK, BLOCK) + t.shape[2:])
    return jnp.moveaxis(t, 1, 0)

def from_blocks(t):
    t = jnp.moveaxis(t, 0, 1)
    return t.reshape((t.shape[0], t.shape[1] * t.shape[2]) + t.shape[3:])

def rope(x, pos):
    half = x.shape[-1] // 2
    freqs = ROPE_THETA ** (-jnp.arange(half, dtype=jnp.float32) / half)
    ang = pos.astype(jnp.float32)[..., None] * freqs
    ang = ang.reshape(ang.shape[:2] + (1,) * (x.ndim - 3) + (half,))
    cos, sin = jnp.cos(ang), jnp.sin(ang)
    x32 = x.astype(jnp.float32)
    x1, x2 = x32[..., :half], x32[..., half:]
    return jnp.concatenate([x1 * cos - x2 * sin, x1 * sin + x2 * cos], axis=-1).astype(x.dtype)

def swa_sink_attention(q, k, v, sinks):
    b, s, h, d = q.shape
    kvh = k.shape[2]
    g = h // kvh
    nb = s // BLOCK
    qb = q.reshape(b, nb, BLOCK, kvh, g, d).astype(jnp.float32)
    kb = k.reshape(b, nb, BLOCK, kvh, d).astype(jnp.float32)
    vb = v.reshape(b, nb, BLOCK, kvh, d).astype(jnp.float32)
    prev = lambda t: jnp.concatenate([jnp.zeros_like(t[:, :1]), t[:, :-1]], axis=1)
    kk = jnp.concatenate([prev(kb), kb], axis=2)
    vv = jnp.concatenate([prev(vb), vb], axis=2)
    scores = jnp.einsum('bnqhgd,bnkhd->bnhgqk', qb, kk) * (d ** -0.5)
    qi = jnp.arange(BLOCK)[:, None]
    kj = jnp.arange(2 * BLOCK)[None, :]
    diff = qi + BLOCK - kj
    blk = jnp.arange(nb)[:, None, None]
    valid = (diff >= 0) & (diff < SWA_WINDOW) & (blk * BLOCK + kj - BLOCK >= 0)
    scores = jnp.where(valid[None, :, None, None], scores, -jnp.inf)
    sink = jnp.broadcast_to(sinks.astype(jnp.float32).reshape(1, 1, kvh, g, 1, 1), scores.shape[:-1] + (1,))
    probs = jax.nn.softmax(jnp.concatenate([scores, sink], axis=-1), axis=-1)[..., :-1]
    out = jnp.einsum('bnhgqk,bnkhd->bnqhgd', probs, vv)
    return out.reshape(b, s, h * d).astype(q.dtype)

def short_gated_conv(bg, cg, xin, conv_w, conv_b):
    u = cg * xin
    y = lax.conv_general_dilated(u, conv_w[:, None, :], window_strides=(1,),
                                 padding=[(CONV_K - 1, 0)],
                                 dimension_numbers=('NWC', 'WIO', 'NWC'),
                                 feature_group_count=u.shape[-1])
    return bg * (y + conv_b)

def causal_softmax_attention(q, k, v):
    b, s, h, dk = q.shape
    scale = dk ** -0.5
    kf = k.astype(jnp.float32)
    vf = v.astype(jnp.float32)
    kpos = jnp.arange(s)

    def step(args):
        qblk, i = args
        sc = jnp.einsum('bqhd,bkhd->bhqk', qblk.astype(jnp.float32), kf) * scale
        qpos = i * BLOCK + jnp.arange(BLOCK)
        sc = jnp.where(kpos[None, :] <= qpos[:, None], sc, -jnp.inf)
        p = jax.nn.softmax(sc, axis=-1)
        return jnp.einsum('bhqk,bkhd->bqhd', p, vf)

    out = lax.map(step, (to_blocks(q), jnp.arange(s // BLOCK)))
    return from_blocks(out).reshape(b, s, -1).astype(q.dtype)

def mla(cq, ckv, kr, pos, g_q, w_uq, g_kv, w_ukv):
    b, s, _ = cq.shape
    q = (rmsnorm(cq, g_q) @ w_uq).reshape(b, s, MLA_HEADS, MLA_NOPE_DIM + MLA_ROPE_DIM)
    q = jnp.concatenate([q[..., :MLA_NOPE_DIM], rope(q[..., MLA_NOPE_DIM:], pos)], axis=-1)
    kv = (rmsnorm(ckv, g_kv) @ w_ukv).reshape(b, s, MLA_HEADS, MLA_NOPE_DIM + MLA_V_DIM)
    k_nope, v = kv[..., :MLA_NOPE_DIM], kv[..., MLA_NOPE_DIM:]
    k_rope = jnp.broadcast_to(rope(kr, pos)[:, :, None, :], (b, s, MLA_HEADS, MLA_ROPE_DIM))
    k = jnp.concatenate([k_nope, k_rope], axis=-1)
    return causal_softmax_attention(q, k, v)

def stick_breaking_attention(q, k, v):
    b, s, h, d = q.shape
    scale = d ** -0.5
    kf = k.astype(jnp.float32)
    vf = v.astype(jnp.float32)
    kpos = jnp.arange(s)

    def step(args):
        qblk, i = args
        z = jnp.einsum('bqhd,bkhd->bhqk', qblk.astype(jnp.float32), kf) * scale
        qpos = i * BLOCK + jnp.arange(BLOCK)
        mask = kpos[None, :] < qpos[:, None]
        log_keep = jnp.where(mask, jax.nn.log_sigmoid(-z), 0.0)
        after = lax.cumsum(log_keep, axis=3, reverse=True) - log_keep
        a = jnp.where(mask, jnp.exp(jax.nn.log_sigmoid(z) + after), 0.0)
        return jnp.einsum('bhqk,bkhd->bqhd', a, vf)

    out = lax.map(step, (to_blocks(q), jnp.arange(s // BLOCK)))
    return from_blocks(out).reshape(b, s, -1).astype(q.dtype)

def hybrid_layer(x, pos, g_pre, w_in, sinks, conv_w, conv_b, g_cq, w_uq, g_ckv, w_ukv, g_grp, w_out, g_post):
    b, s, _ = x.shape
    h = rmsnorm(x, g_pre) @ w_in
    (a_q, a_k, a_v, b_b, b_c, b_x, c_q, c_kv, c_kr, d_q, d_k, d_v, gate) = jnp.split(h, SPLIT_IDX, axis=-1)
    ya = swa_sink_attention(a_q.reshape(b, s, SWA_HEADS, SWA_HEAD_DIM),
                            a_k.reshape(b, s, SWA_KV_HEADS, SWA_HEAD_DIM),
                            a_v.reshape(b, s, SWA_KV_HEADS, SWA_HEAD_DIM), sinks)
    yb = short_gated_conv(b_b, b_c, b_x, conv_w, conv_b)
    yc = mla(c_q, c_kv, c_kr, pos, g_cq, w_uq, g_ckv, w_ukv)
    yd = stick_breaking_attention(d_q.reshape(b, s, SB_HEADS, SB_HEAD_DIM),
                                  d_k.reshape(b, s, SB_HEADS, SB_HEAD_DIM),
                                  d_v.reshape(b, s, SB_HEADS, SB_HEAD_DIM))
    y = jnp.stack([ya, yb, yc, yd], axis=2)
    y = rmsnorm(y, g_grp.reshape(N_GROUPS, GROUP_WIDTH)).reshape(b, s, D_MIX)
    y = y * jax.nn.silu(gate)
    return x + rmsnorm(y @ w_out, g_post)

def first_inputs(seed: int = 0) -> dict:
    key = jax.random.key(seed)
    ks = jax.random.split(key, 16)
    f32 = jnp.float32
    nrm = lambda k, shape, scale: jax.random.normal(k, shape, f32) * scale
    gain = lambda k, shape: 1.0 + 0.02 * jax.random.normal(k, shape, f32)
    x = jax.random.normal(ks[0], (BATCH, SEQ, D_MODEL), f32)
    positions = jnp.broadcast_to(jnp.arange(SEQ, dtype=jnp.int32)[None, :], (BATCH, SEQ))
    return {
        "x": x,
        "positions": positions,
        "norm_pre": gain(ks[1], (DEPTH, D_MODEL)),
        "w_in": nrm(ks[2], (DEPTH, D_MODEL, D_IN), D_MODEL ** -0.5),
        "attn_sinks": nrm(ks[3], (DEPTH, SWA_HEADS), 0.5),
        "conv_w": nrm(ks[4], (DEPTH, CONV_K, CONV_WIDTH), CONV_K ** -0.5),
        "conv_b": nrm(ks[5], (DEPTH, CONV_WIDTH), 0.01),
        "mla_q_norm": gain(ks[6], (DEPTH, MLA_Q_RANK)),
        "mla_w_uq": nrm(ks[7], (DEPTH, MLA_Q_RANK, MLA_HEADS * (MLA_NOPE_DIM + MLA_ROPE_DIM)), MLA_Q_RANK ** -0.5),
        "mla_kv_norm": gain(ks[8], (DEPTH, MLA_KV_RANK)),
        "mla_w_ukv": nrm(ks[9], (DEPTH, MLA_KV_RANK, MLA_HEADS * (MLA_NOPE_DIM + MLA_V_DIM)), MLA_KV_RANK ** -0.5),
        "group_norm": gain(ks[10], (DEPTH, D_MIX)),
        "w_out": nrm(ks[11], (DEPTH, D_MIX, D_MODEL), D_MIX ** -0.5),
        "norm_post": gain(ks[12], (DEPTH, D_MODEL)),
    }

def first_block(x, positions, norm_pre, w_in, attn_sinks, conv_w, conv_b, mla_q_norm, mla_w_uq,
              mla_kv_norm, mla_w_ukv, group_norm, w_out, norm_post):
    for l in range(DEPTH):
        x = hybrid_layer(x, positions, norm_pre[l], w_in[l], attn_sinks[l], conv_w[l], conv_b[l],
                         mla_q_norm[l], mla_w_uq[l], mla_kv_norm[l], mla_w_ukv[l],
                         group_norm[l], w_out[l], norm_post[l])
    return x


GRID_W = 64
CTX_LEN = 256
HEAD_DIM = 64
ATTN_W = D_MODEL // 2
N_Q_HEADS = ATTN_W // HEAD_DIM
N_KV_HEADS = max(1, N_Q_HEADS // 4)
GQA_GROUP = N_Q_HEADS // N_KV_HEADS
KV_W = N_KV_HEADS * HEAD_DIM
ROPE_AXIS_DIM = HEAD_DIM // 2
Q_BLOCK = 128
FOURIER_W = D_MODEL // 4
FOURIER_GROUPS = 4
FOURIER_GROUP_DIM = FOURIER_W // FOURIER_GROUPS
HYENA_W = D_MODEL - ATTN_W - FOURIER_W
HYENA_BANDS = 16
HYENA_EMB = 1 + 2 * HYENA_BANDS
HYENA_FILTER_W = 64
HYENA_FAST_DECAY = 0.3
HYENA_SLOW_DECAY = 1.5
HYENA_TARGET = 1e-2
MIX_W = ATTN_W + FOURIER_W + HYENA_W
Q0 = 0
K0 = ATTN_W
V0 = K0 + KV_W
F0 = V0 + KV_W
H0 = F0 + FOURIER_W
IN_W = H0 + 3 * HYENA_W
D_FF = int(math.ceil(8 * D_MODEL / 3 / 128)) * 128


def rmsnorm_2(x, g):
    xf = x.astype(jnp.float32)
    y = xf * lax.rsqrt(jnp.mean(xf * xf, axis=-1, keepdims=True) + NORM_EPS)
    return (y * g.astype(jnp.float32)).astype(x.dtype)

def dwconv3(u, w, b):
    up = jnp.pad(u, ((0, 0), (1, 1), (0, 0)))
    return up[:, :-2] * w[0] + up[:, 1:-1] * w[1] + up[:, 2:] * w[2] + b

def rope2d(x, ang_r, ang_c):
    def rot(xa, ang):
        cos = jnp.cos(ang)[:, None, :].astype(xa.dtype)
        sin = jnp.sin(ang)[:, None, :].astype(xa.dtype)
        x1, x2 = jnp.split(xa, 2, axis=-1)
        return jnp.concatenate([x1 * cos - x2 * sin, x2 * cos + x1 * sin], axis=-1)
    xr, xc = jnp.split(x, 2, axis=-1)
    return jnp.concatenate([rot(xr, ang_r), rot(xc, ang_c)], axis=-1)

def attend(q, k, v):
    s = jnp.einsum('bqhgd,bkhd->bhgqk', q, k).astype(jnp.float32) * (HEAD_DIM ** -0.5)
    p = jax.nn.softmax(s, axis=-1).astype(v.dtype)
    return jnp.einsum('bhgqk,bkhd->bqhgd', p, v)

def blocked_attention(q, k, v):
    B, L = q.shape[0], q.shape[1]
    nb = L // Q_BLOCK
    qb = q.reshape(B, nb, Q_BLOCK, N_KV_HEADS, GQA_GROUP, HEAD_DIM).swapaxes(0, 1)
    ob = lax.map(lambda qq: attend(qq, k, v), qb)
    return ob.swapaxes(0, 1).reshape(B, L, ATTN_W)

def fourier_mix(f, w):
    B, L, _ = f.shape
    fg = f.astype(jnp.float32).reshape(B, L, FOURIER_GROUPS, FOURIER_GROUP_DIM)
    y = jnp.fft.fft2(fg, axes=(1, 3), norm='ortho').real.astype(f.dtype)
    return y.reshape(B, L, FOURIER_W) @ w

def hyena_filter(L, w1, b1, fr1, w2, b2, fr2, w3):
    f32 = jnp.float32
    t = jnp.linspace(0.0, 1.0, L, dtype=f32)[:, None]
    bands = jnp.linspace(1e-4, HYENA_BANDS - 1, HYENA_BANDS, dtype=f32)
    ang = (2.0 * math.pi) * jnp.arange(L, dtype=f32)[:, None] / L * bands[None, :]
    z = jnp.concatenate([t, jnp.cos(ang), -jnp.sin(ang)], axis=-1)
    h = jnp.sin(fr1.astype(f32) * (z @ w1.astype(f32) + b1.astype(f32)))
    h = jnp.sin(fr2.astype(f32) * (h @ w2.astype(f32) + b2.astype(f32)))
    h = h @ w3.astype(f32)
    deltas = jnp.abs(jnp.linspace(math.log(HYENA_TARGET) / HYENA_SLOW_DECAY,
                                  math.log(HYENA_TARGET) / HYENA_FAST_DECAY, HYENA_W, dtype=f32))
    decay = jnp.exp(-t * deltas[None, :])
    h_fwd = h[:, :HYENA_W] * decay
    h_bwd = h[:, HYENA_W:] * decay
    two = jnp.concatenate([h_fwd, jnp.zeros((1, HYENA_W), f32), h_bwd[:0:-1]], axis=0)
    return two / jnp.sum(jnp.abs(two), axis=0, keepdims=True)

def hyena_longconv(u, filt, bias):
    L = u.shape[1]
    n = 2 * L
    uf = jnp.fft.rfft(u.astype(jnp.float32), n=n, axis=1)
    kf = jnp.fft.rfft(filt, n=n, axis=0)
    y = jnp.fft.irfft(uf * kf[None], n=n, axis=1)[:, :L]
    return (y + u.astype(jnp.float32) * bias.astype(jnp.float32)).astype(u.dtype)

def hyena_mix(p, conv_w, conv_b, filt, bias):
    uc = dwconv3(p, conv_w, conv_b)
    x0, x1, v = jnp.split(uc, 3, axis=-1)
    return x0 * hyena_longconv(x1 * v, filt, bias)

def conv_ffn(h, w_up, w_c, b_c, w_down):
    u = dwconv3(h @ w_up, w_c, b_c)
    gate, val = jnp.split(u, 2, axis=-1)
    return (jax.nn.silu(gate) * val) @ w_down

def second_inputs(seed: int = 0) -> dict:
    key = jax.random.key(seed)
    ks = jax.random.split(key, 32)
    f32 = jnp.float32

    def nrm(k, shape, scale):
        return jax.random.normal(k, shape, f32) * scale

    def gain(k, shape):
        return 1.0 + 0.05 * jax.random.normal(k, shape, f32)

    return {
        'x': nrm(ks[0], (BATCH, SEQ, D_MODEL), 1.0),
        'c': nrm(ks[1], (BATCH, D_MODEL), 1.0),
        'ctx': nrm(ks[2], (BATCH, CTX_LEN, D_MODEL), 1.0),
        'c_ctx': nrm(ks[3], (D_MODEL,), 1.0),
        'w_mod': nrm(ks[4], (DEPTH, D_MODEL, 6 * D_MODEL), 0.5 * D_MODEL ** -0.5),
        'b_mod': nrm(ks[5], (DEPTH, 6 * D_MODEL), 0.02),
        'g_pre_mix': gain(ks[6], (DEPTH, D_MODEL)),
        'g_post_mix': gain(ks[7], (DEPTH, D_MODEL)),
        'g_pre_ffn': gain(ks[8], (DEPTH, D_MODEL)),
        'g_post_ffn': gain(ks[9], (DEPTH, D_MODEL)),
        'w_in': nrm(ks[10], (DEPTH, D_MODEL, IN_W), D_MODEL ** -0.5),
        'g_q': gain(ks[11], (DEPTH, HEAD_DIM)),
        'g_k': gain(ks[12], (DEPTH, HEAD_DIM)),
        'w_fourier': nrm(ks[13], (DEPTH, FOURIER_W, FOURIER_W), FOURIER_W ** -0.5),
        'w_hy_conv': nrm(ks[14], (DEPTH, 3, 3 * HYENA_W), 3 ** -0.5),
        'b_hy_conv': nrm(ks[15], (DEPTH, 3 * HYENA_W), 0.02),
        'hy_w1': nrm(ks[16], (DEPTH, HYENA_EMB, HYENA_FILTER_W), HYENA_EMB ** -0.5),
        'hy_b1': nrm(ks[17], (DEPTH, HYENA_FILTER_W), 0.1),
        'hy_fr1': gain(ks[18], (DEPTH, HYENA_FILTER_W)),
        'hy_w2': nrm(ks[19], (DEPTH, HYENA_FILTER_W, HYENA_FILTER_W), HYENA_FILTER_W ** -0.5),
        'hy_b2': nrm(ks[20], (DEPTH, HYENA_FILTER_W), 0.1),
        'hy_fr2': gain(ks[21], (DEPTH, HYENA_FILTER_W)),
        'hy_w3': nrm(ks[22], (DEPTH, HYENA_FILTER_W, 2 * HYENA_W), HYENA_FILTER_W ** -0.5),
        'hy_bias': nrm(ks[23], (DEPTH, HYENA_W), 0.1),
        'w_out': nrm(ks[24], (DEPTH, MIX_W, D_MODEL), MIX_W ** -0.5),
        'w_up': nrm(ks[25], (DEPTH, D_MODEL, 2 * D_FF), D_MODEL ** -0.5),
        'w_ffn_conv': nrm(ks[26], (DEPTH, 3, 2 * D_FF), 3 ** -0.5),
        'b_ffn_conv': nrm(ks[27], (DEPTH, 2 * D_FF), 0.02),
        'w_down': nrm(ks[28], (DEPTH, D_FF, D_MODEL), D_FF ** -0.5),
    }

def second_block(x, c, ctx, c_ctx, w_mod, b_mod, g_pre_mix, g_post_mix, g_pre_ffn, g_post_ffn,
              w_in, g_q, g_k, w_fourier, w_hy_conv, b_hy_conv, hy_w1, hy_b1, hy_fr1,
              hy_w2, hy_b2, hy_fr2, hy_w3, hy_bias, w_out, w_up, w_ffn_conv, b_ffn_conv, w_down):
    B, L, _ = x.shape
    C = ctx.shape[1]
    ROWS = L // GRID_W
    row = jnp.repeat(jnp.arange(ROWS, dtype=jnp.float32), GRID_W)
    col = jnp.tile(jnp.arange(GRID_W, dtype=jnp.float32), ROWS)
    inv = ROPE_THETA ** (-jnp.arange(0, ROPE_AXIS_DIM, 2, dtype=jnp.float32) / ROPE_AXIS_DIM)
    ang_r = row[:, None] * inv[None, :]
    ang_c = col[:, None] * inv[None, :]

    for i in range(DEPTH):
        last = i == DEPTH - 1
        mod_x = (jax.nn.silu(c) @ w_mod[i] + b_mod[i])[:, None, :]
        mod_c = (jax.nn.silu(c_ctx) @ w_mod[i] + b_mod[i])[None, None, :]
        sh1, sc1, ga1, sh2, sc2, ga2 = jnp.split(mod_x, 6, axis=-1)
        csh1, csc1, cga1, csh2, csc2, cga2 = jnp.split(mod_c, 6, axis=-1)
        hy_params = (hy_w1[i], hy_b1[i], hy_fr1[i], hy_w2[i], hy_b2[i], hy_fr2[i], hy_w3[i])

        hx = rmsnorm_2(x, g_pre_mix[i]) * (1.0 + sc1) + sh1
        hc = rmsnorm_2(ctx, g_pre_mix[i]) * (1.0 + csc1) + csh1
        px = hx @ w_in[i]
        pc = hc @ (w_in[i][:, K0:F0] if last else w_in[i])
        pc_kv = pc if last else pc[..., K0:F0]

        kc = rmsnorm_2(pc_kv[..., :KV_W].reshape(B, C, N_KV_HEADS, HEAD_DIM), g_k[i])
        vc = pc_kv[..., KV_W:].reshape(B, C, N_KV_HEADS, HEAD_DIM)
        q = rope2d(rmsnorm_2(px[..., Q0:K0].reshape(B, L, N_Q_HEADS, HEAD_DIM), g_q[i]), ang_r, ang_c)
        k = rope2d(rmsnorm_2(px[..., K0:V0].reshape(B, L, N_KV_HEADS, HEAD_DIM), g_k[i]), ang_r, ang_c)
        v = px[..., V0:F0].reshape(B, L, N_KV_HEADS, HEAD_DIM)
        k_all = jnp.concatenate([kc, k], axis=1)
        v_all = jnp.concatenate([vc, v], axis=1)
        attn_x = blocked_attention(q.reshape(B, L, N_KV_HEADS, GQA_GROUP, HEAD_DIM), k_all, v_all)
        four_x = fourier_mix(px[..., F0:H0], w_fourier[i])
        hy_x = hyena_mix(px[..., H0:], w_hy_conv[i], b_hy_conv[i], hyena_filter(L, *hy_params), hy_bias[i])
        mix_x = jnp.concatenate([attn_x, four_x, hy_x], axis=-1) @ w_out[i]
        x = x + ga1 * rmsnorm_2(mix_x, g_post_mix[i])

        if not last:
            qc = rmsnorm_2(pc[..., Q0:K0].reshape(B, C, N_Q_HEADS, HEAD_DIM), g_q[i])
            attn_c = attend(qc.reshape(B, C, N_KV_HEADS, GQA_GROUP, HEAD_DIM), kc, vc).reshape(B, C, ATTN_W)
            four_c = fourier_mix(pc[..., F0:H0], w_fourier[i])
            hy_c = hyena_mix(pc[..., H0:], w_hy_conv[i], b_hy_conv[i], hyena_filter(C, *hy_params), hy_bias[i])
            mix_c = jnp.concatenate([attn_c, four_c, hy_c], axis=-1) @ w_out[i]
            ctx = ctx + cga1 * rmsnorm_2(mix_c, g_post_mix[i])

        fx = rmsnorm_2(x, g_pre_ffn[i]) * (1.0 + sc2) + sh2
        yx = conv_ffn(fx, w_up[i], w_ffn_conv[i], b_ffn_conv[i], w_down[i])
        x = x + ga2 * rmsnorm_2(yx, g_post_ffn[i])
        if not last:
            fc = rmsnorm_2(ctx, g_pre_ffn[i]) * (1.0 + csc2) + csh2
            yc = conv_ffn(fc, w_up[i], w_ffn_conv[i], b_ffn_conv[i], w_down[i])
            ctx = ctx + cga2 * rmsnorm_2(yc, g_post_ffn[i])

    return x


def setup_inputs(seed=0):
    out = dict(first_inputs(seed))
    for name, value in second_inputs(seed + 1).items():
        if name != "x":
            out[name + "_2"] = value
    return out


def reference(
    x, positions, norm_pre, w_in, attn_sinks, conv_w, conv_b, mla_q_norm, mla_w_uq, mla_kv_norm,
    mla_w_ukv, group_norm, w_out, norm_post, c_2, ctx_2, c_ctx_2, w_mod_2, b_mod_2, g_pre_mix_2,
    g_post_mix_2, g_pre_ffn_2, g_post_ffn_2, w_in_2, g_q_2, g_k_2, w_fourier_2, w_hy_conv_2,
    b_hy_conv_2, hy_w1_2, hy_b1_2, hy_fr1_2, hy_w2_2, hy_b2_2, hy_fr2_2, hy_w3_2, hy_bias_2,
    w_out_2, w_up_2, w_ffn_conv_2, b_ffn_conv_2, w_down_2,
):
    x = first_block(
        x, positions, norm_pre, w_in, attn_sinks, conv_w, conv_b, mla_q_norm, mla_w_uq,
        mla_kv_norm, mla_w_ukv, group_norm, w_out, norm_post,
    )
    return second_block(
        x, c_2, ctx_2, c_ctx_2, w_mod_2, b_mod_2, g_pre_mix_2, g_post_mix_2, g_pre_ffn_2,
        g_post_ffn_2, w_in_2, g_q_2, g_k_2, w_fourier_2, w_hy_conv_2, b_hy_conv_2, hy_w1_2,
        hy_b1_2, hy_fr1_2, hy_w2_2, hy_b2_2, hy_fr2_2, hy_w3_2, hy_bias_2, w_out_2, w_up_2,
        w_ffn_conv_2, b_ffn_conv_2, w_down_2,
    )


_drawn_inputs = setup_inputs


def setup_inputs(seed=0):
    import zlib

    import numpy as np

    out = dict(_drawn_inputs(seed))
    spreads = {}
    factors = {'attn_sinks': 5.289,
     'conv_b': 8.0,
     'mla_q_norm': 5.051,
     'mla_kv_norm': 3.468,
     'ctx_2': 3.787,
     'g_pre_mix_2': 4.657,
     'g_post_mix_2': 4.634,
     'g_pre_ffn_2': 3.259,
     'g_post_ffn_2': 4.749,
     'g_q_2': 8.0,
     'g_k_2': 8.0,
     'b_hy_conv_2': 8.0,
     'hy_b1_2': 8.0,
     'hy_fr1_2': 8.0,
     'hy_b2_2': 7.226,
     'hy_fr2_2': 8.0,
     'b_ffn_conv_2': 8.0}
    for name, (base, spread) in spreads.items():
        noise = np.random.default_rng([zlib.crc32(name.encode()), seed]).standard_normal(out[name].shape)
        drawn = base * np.exp(spread * noise) if base else spread * noise
        out[name] = jnp.asarray(drawn.astype(out[name].dtype))
    for name, factor in factors.items():
        out[name] = (out[name] * factor).astype(out[name].dtype)
    return out
```

```python
from contextlib import ExitStack

import concourse.bass as bass
from concourse import mybir
from concourse.alu_op_type import AluOpType as ALU

F32 = mybir.dt.float32
I32 = mybir.dt.int32
ACT = mybir.ActivationFunctionType
AX_X = mybir.AxisListType.X

P = 128
D = 1024
KD = D // P
DEPTH = 2
EPS = 1e-6
LNEXP = "natural_log_exp_and_others"

T = 512
NT = T // P
A_H, A_D = 4, 64
M_H, M_N, M_R = 4, 64, 32
M_K = M_N + M_R
AQ, AK, AV, CQ, CKV, DQ, DK, DV, BB, BC, BX, GATE = 0, 2, 3, 4, 6, 7, 9, 11, 13, 15, 17, 19
NH = 27
R1 = 5
W1N = NH + KD
RM, MODN = 3, 48
P_PRE, P_POST, P_GRP, P_CW, P_CB, P_GCQ, P_GCKV, P_SINK, NP1 = 0, 8, 16, 24, 30, 32, 34, 35, 39
C_ONES, C_BD, C_ID, C_NTRI, C_NONE, C_SWAP, C_CAUS, C_PREV, C_FREQ, C_SW2, C_FD, C_END = (
    0, 128, 256, 384, 512, 640, 672, 800, 928, 932, 1060, 1316)

R2 = 4
LC = 256
Q_H, KV_H, H_D = 8, 2, 64
FK = 22
W2N = 14 + KD + 2 * FK + FK
(P_GPM, P_GPOM, P_GPF, P_GPOF, P_GQ, P_GK, P_HCW, P_HCB, P_B1, P_FR1, P_B2, P_FR2, P_HB,
 P_FCW, P_FCB, P_W1, P_W2, P_W3, NP2) = (
    0, 8, 16, 24, 32, 33, 34, 52, 58, 59, 60, 61, 62, 64, 196, 240, 304, 368, 880)
FSTART = 1
INV_2PI = 0.15915494309189535
MAGIC = 12582912.0
TP_A, TP_B, TP_C = 6.28125, 0.0019340515136718750, 1.2556659146e-06
PI = 3.14159274
HALF_PI = 1.5707963267948966


class Link:

    def __init__(self, eng, sem, base):
        self.eng, self.sem, self.base, self.n = eng, sem, base, 0

    def __call__(self, ins):
        ins.then_inc(self.sem, 1)
        self.n += 1
        self.eng.wait_ge(self.sem, self.base + self.n)


PER1 = dict(
    params=32, x_squared=KD, x_summed=1, sum_read=8, rstd_ready=8, xn_ready=KD, mod_used=MODN,
    acc_ready=44, acc0_free=22, acc1_free=22, kr_ready=1, lat_squared=3, lat_summed=2, lat_ready=3,
    qc_in=4, kvc_in=4, kr_in=1, swap_ready=5, rot_ready=5, kr_copied=4,
    vt_ready=8, vt_copied=8, sc_ready=32, negmax=32, p_exp=32, p_norm=32, pt_ready=32, pt_copied=32,
    o_ready=32, o_copied=32, z_ready=16, z_ln=16, sp_done=16, sp_masked=16, wz_ready=16, a_exp=16,
    a_masked=16, sbo_ready=4, sbo_copied=4, conv_done=2, y_squared=8, y_summed=4, y_normed=8,
    gate_sig=8, gate_mul=8, y_ready=8, z_squared=KD, z_summed=1, zn_ready=KD, x_updated=KD,
    mod_copied=1, link_act=48, link_dve=93, link_pool=0,
)


START = dict(x_updated=1, sum_read=1, acc0_free=1, acc1_free=1, rot_ready=1, mod_copied=1)


def counts2(blocks, queries_ctx):
    tiles = Q_H * blocks
    return dict(
        loaded2=64, tables_f=32, tables_h=32, md_ready=1, x2_squared=16, x2_summed=2, sum2_read=9, rstd2=9,
        xs2=16, xn2=16, acc2=80, acc2_0_free=40, acc2_1_free=40, down_used=20,
        hn_squared=5, hn_summed=5, hn_normed=5, turn_ready=5, hn_turned=5, v2_ready=blocks, v2_copied=blocks,
        flt_in=2, flt_arg=2, flt_sin=2, flt_h=blocks, flt_decayed=blocks, flt_sums=1, flt_abs=1, flt_norm=1,
        flt_inv=1, spec_ready=blocks, spec_copied=blocks, four_ready=blocks, four_copied=blocks,
        conv_mid=50, conv2=50, u_ready=2, ut_ready=blocks, ut_copied=blocks, us_ready=blocks, us_mul=blocks,
        us_done=blocks, hy_out=2, sc2=tiles, neg2=tiles, pe2=tiles, pn2=tiles, pt2=tiles, pc2=tiles,
        pd2=0 if queries_ctx else tiles, o2=tiles, oc2=tiles, z2_squared=16, z2_summed=2, zn2=16, x2_updated=16,
        gate_sig2=FK, gate_mul2=FK, g_ready=FK, link2_dve=LINK_DVE2[queries_ctx],
    )


LINK_DVE2 = {True: 61, False: 93}
START2 = dict(g_ready=2)


def product_of(j):
    return j if j < DQ else j + 1 if j < BB + 2 else j + 9


def tiles1():
    return [("a", h, i) for i in range(NT) for h in range(A_H)] + [("m", h, i) for i in range(NT) for h in range(M_H)]


def build(nc, x_in, ctx_in, pos, w1, mla_w, p1, consts, wmod, modp, w2, p2, tables, tabs_c, rope2, out):
    with ExitStack() as ctx:
        def sb(name, n, dt=F32, parts=P):
            return ctx.enter_context(nc.sbuf_tensor(name, [parts, n], dt))

        ps_t = ctx.enter_context(nc.psum_tensor("banks", [P, 8 * 512], F32))
        ps = [ps_t[:, i * 512:(i + 1) * 512] for i in range(8)]
        names = list(PER1)
        sm = {n: ctx.enter_context(nc.semaphore(n)) for n in names}
        w_landed = [ctx.enter_context(nc.semaphore(f"w_landed{s}")) for s in range(R1)]
        mod_landed = [ctx.enter_context(nc.semaphore(f"mod_landed{s}")) for s in range(RM)]
        PC, PX = counts2(LC // P, True), counts2(NT, False)
        sm2 = {n: ctx.enter_context(nc.semaphore(n)) for n in PX}
        w2_landed = [ctx.enter_context(nc.semaphore(f"w2_landed{s}")) for s in range(R2)]
        KV1 = ("kv_loaded", "kv_md", "kv_squared", "kv_summed", "kv_rstd", "kv_xs", "kv_xn", "kv_acc", "kv_taken",
               "kv_ksq", "kv_ksum", "kv_krstd", "kv_tr", "kv_done", "kv_link")
        sk = {n: ctx.enter_context(nc.semaphore(n)) for n in KV1}
        tables_u = [ctx.enter_context(nc.semaphore(f"tables_u{i}")) for i in range(2)]
        conv_left = [ctx.enter_context(nc.semaphore(f"conv_left{i}")) for i in range(2)]
        pool_chain = ctx.enter_context(nc.semaphore("pool_chain"))
        kv_chain = ctx.enter_context(nc.semaphore("kv_chain"))
        ctx_loaded = ctx.enter_context(nc.semaphore("ctx_loaded"))
        x_loaded = ctx.enter_context(nc.semaphore("x_loaded"))
        consts_loaded = ctx.enter_context(nc.semaphore("consts_loaded"))
        waits_passed = ctx.enter_context(nc.semaphore("waits_passed"))
        small_set = ctx.enter_context(nc.semaphore("small_set"))
        rope_ready = ctx.enter_context(nc.semaphore("rope_ready"))
        link_rope = ctx.enter_context(nc.semaphore("link_rope"))
        sin_in = ctx.enter_context(nc.semaphore("sin_in"))
        out_written = ctx.enter_context(nc.semaphore("out_written"))

        x_t = sb("x_t", KD * 512)
        xn_t = sb("xn_t", KD * 512)
        ring_t = sb("ring", R1 * 1024)
        mring_t = sb("mring", RM * 1024)
        big = sb("big", 28 * 512)
        y_t = sb("y_t", KD * 512)
        cst = sb("cst", C_END)
        par = sb("par", NP1)
        mw = sb("mw", 1536)
        mods = sb("mods", DEPTH * 96)
        modp_t = sb("modp_t", DEPTH * 96 + 16)
        cv = sb("cv", 32)
        eps_t = sb("eps_t", 2)
        rstd_t = sb("rstd_t", 2 * 512)
        sq_t = sb("sq_t", 4 * 512)
        qh_t = sb("qh_t", M_H * 512)
        kh_t = sb("kh_t", M_H * 512)
        va_t = sb("va_t", NT * P)
        vm_t = sb("vm_t", NT * 256)
        vd_t = sb("vd_t", NT * 256)
        prob_t = sb("prob_t", 2048)
        pr_t, pt_t = prob_t[:, 0:1024], prob_t[:, 1024:2048]
        sp_t = xn_t[:, 0:2560]
        a_t = xn_t[:, 2560:3840]
        lz_t = pr_t
        cs_t = sb("cs_t", 2 * 512)
        rot_t = sb("rot_t", 512)
        st_t = sb("st_t", 5 * 32)
        pos_t = y_t[:, 0:512].bitcast(I32)

        X = [x_t[:, c * 512:(c + 1) * 512] for c in range(KD)]
        XN = [xn_t[:, c * 512:(c + 1) * 512] for c in range(KD)]
        H = [big[:, c * 512:(c + 1) * 512] for c in range(28)]
        Y = [y_t[:, c * 512:(c + 1) * 512] for c in range(KD)]
        Z = XN
        RING = [ring_t[:, s * 1024:(s + 1) * 1024] for s in range(R1)]
        MRING = [mring_t[:, s * 1024:(s + 1) * 1024] for s in range(RM)]
        SQ = [sq_t[:, c * 512:(c + 1) * 512] for c in range(4)]
        RSTD = [rstd_t[:, c * 512:(c + 1) * 512] for c in range(2)]
        QH = [qh_t[:, h * 512:(h + 1) * 512] for h in range(M_H)]
        KH = [kh_t[:, h * 512:(h + 1) * 512] for h in range(M_H)]
        VM_IN = [Y[4 + h] for h in range(M_H)]
        ROT = [rot_t[:], y_t[:, 512:1024]]
        COS, SIN = cs_t[64:96, 0:512], cs_t[64:96, 512:1024]
        LZ = [lz_t[:, b * 512:(b + 1) * 512] for b in range(2)]
        ones, bd, ident = cst[:, C_ONES:C_ONES + P], cst[:, C_BD:C_BD + P], cst[:, C_ID:C_ID + P]
        ntri, nones = cst[:, C_NTRI:C_NTRI + P], cst[:, C_NONE:C_NONE + P]
        eps, one = eps_t[:, 0:1], eps_t[:, 1:2]
        KR = H[27]

        def pcol(c):
            return par[:, c:c + 1]

        par2 = sb("par2", NP2 + 512)
        md = sb("md", 80)
        ninv = sb("ninv", 2)
        KCS, VCS = vd_t[:, 0:2 * LC], vd_t[:, 2 * LC:4 * LC]
        KALL, VALL = kh_t[:, 0:768], kh_t[:, 768:1536]
        TABC, TABS = qh_t[:], mring_t[:, 0:2048]
        SPEC = [ring_t[:, 4096:5120], mring_t[:, 2048:3072]]
        RING2 = [ring_t[:, s * 1024:(s + 1) * 1024] for s in range(R2)]
        G1, GA1, G2, GA2 = 48, 56, 64, 72
        SH1, SC1, GT1, SH2, SC2, GT2 = 0, 8, 16, 24, 32, 40

        def p2c(c, rows=slice(0, P)):
            return par2[rows, c:c + 1]

        def view2(is_ctx):
            n = LC if is_ctx else T
            def cut(t, count, base=0):
                return [t[:, base + c * n:base + (c + 1) * n] for c in range(count)]
            b = n // P
            return dict(
                L=n, B=b, X=cut(xn_t, KD, 2048) if is_ctx else X, XN=cut(xn_t, KD), Y=cut(y_t, KD), PX=cut(big, 8),
                H=cut(big, 28), UC=cut(big, 6, 8 * n), G=cut(big, FK), AG=cut(big, 2, 22 * n), AV=cut(big, 2, 24 * n),
                SG=cut(big, 2, 26 * n), HF=[big[:, 14 * n + i * 512:14 * n + (i + 1) * 512] for i in range(b)],
                HP=[big[:, 18 * n + i * 256:18 * n + (i + 1) * 256] for i in range(b)],
                HM=[big[:, 20 * n + i * 256:20 * n + (i + 1) * 256] for i in range(b)],
                DEC=[big[:, 22 * n + i * 512:22 * n + (i + 1) * 512] for i in range(b)],
                ZT=big[0:33, 26 * n:27 * n], H12=big[0:64, 27 * n:28 * n],
                FG=[big[:, 14 * n + i * 512:14 * n + (i + 1) * 512] for i in range(b)],
                UT=[big[:, 26 * n + i * 256:26 * n + (i + 1) * 256] for i in range(b)],
                YR=[big[:, 14 * n + i * 512:14 * n + i * 512 + 256] for i in range(b)],
                YI=[big[:, 14 * n + i * 512 + 256:14 * n + (i + 1) * 512] for i in range(b)],
                UM=[big[:, 22 * n + i * 512:22 * n + (i + 1) * 512] for i in range(b)],
                SPEC=[SPEC[i // 2][:, (i % 2) * 512:(i % 2 + 1) * 512] for i in range(b)],
                TC=[TABC[:, i * n:(i + 1) * n] for i in range(b)], TS=[TABS[:, i * n:(i + 1) * n] for i in range(b)],
                COS=cs_t[:, 0:n], SIN=cs_t[:, 512:512 + n], ROT=rot_t[:, 0:n], SQ=[sq_t[:, i * n:(i + 1) * n] for i in range(4)],
                K=KCS[:, 0:LC] if is_ctx else KALL, KNEW=KCS[:, 0:LC] if is_ctx else KALL[:, LC:LC + T],
                V=[VCS[:, i * P:(i + 1) * P] for i in range(b)] if is_ctx else [VALL[:, i * P:(i + 1) * P] for i in range(6)],
                V0=0 if is_ctx else LC // P, W=LC if is_ctx else LC + T,
                tiles=[(i, j, half) for i in range(b) for j in range(4) for half in range(2)],
                which=1 if is_ctx else 0, RSTD=[RSTD[i][:, 0:n] for i in range(2)],
                PR=[prob_t[:, 0:768], prob_t[:, 768:1536]], PT=[sq_t[:, 0:768], sq_t[:, 768:1536]], first=0 if is_ctx else W2N + 2,
            )

        def at2_of(is_ctx, l):
            def at2(name, i):
                i += START2.get(name, 0)
                return sm2[name], i if is_ctx else l * PX[name] + PC[name] + i
            def landed2(j, g=0):
                n = (0 if is_ctx else W2N + 2) + j
                turn = g + n // R2 + 1
                return w2_landed[n % R2], 16 * (turn if is_ctx else l * (W2N // R2) + turn)
            def slot2(j):
                return RING2[((0 if is_ctx else W2N + 2) + j) % R2]
            return at2, landed2, slot2

        def tile(i):
            kind, h, b = TILES[i]
            qs = slice(b * P, (b + 1) * P)
            if kind == "a":
                kv, r = h // 2, slice(64 * (h // 2), 64 * (h // 2) + 64)
                k0 = max(b - 1, 0)
                mask = cst[:, C_CAUS:C_CAUS + P] if b == 0 else cst[:, C_CAUS:C_CAUS + 2 * P]
                return dict(q=H[AQ + h % 2][r, qs], k=H[AK][r, k0 * P:(b + 1) * P], n=b + 1 - k0, k0=k0, kind=kind,
                            v=lambda j: va_t[:, j * P + 64 * kv:j * P + 64 * kv + 64], h=h, b=b, y=Y[h // 2],
                            base=64 * (h % 2))
            return dict(q=QH[h][0:M_K, qs], k=KH[h][0:M_K, 0:(b + 1) * P], n=b + 1, k0=0, kind=kind,
                        v=lambda j: vm_t[:, j * 256 + 64 * h:j * 256 + 64 * h + 64], h=h, b=b, y=Y[4 + h // 2],
                        base=64 * (h % 2))

        TILES = tiles1()
        TN = len(TILES)
        M_SCALE = float(M_K) ** -0.5
        OFF = [sum(512 - P * j for j in range(k)) for k in range(NT)]

        def units():
            return [(h, k) for h in range(4) for k in reversed(range(NT))]

        block = ctx.enter_context(nc.Block())

        @block.sync
        def _(sp):
            sp.dma_start(cst[:], consts).then_inc(consts_loaded, 16)
            sp.dma_start(modp_t[:], modp).then_inc(consts_loaded, 16)
            sp.dma_start(pos_t[64:96, :], pos).then_inc(consts_loaded, 16)
            sp.dma_start(x_t[:].rearrange("p (c t) -> p c t", c=KD), x_in.rearrange("c p t -> p c t")).then_inc(x_loaded, 16)
            with sp.Fori(0, DEPTH) as l:
                def at(name, i):
                    return sm[name], l * PER1[name] + i + START.get(name, 0)
                sp.wait_ge(*at("x_updated", 0))
                sp.dma_start(par[:], p1[l]).then_inc(sm["params"], 16)
                sp.dma_start(mw[:], mla_w[l]).then_inc(sm["params"], 16)
                for j in range(W1N):
                    if j >= R1:
                        sp.wait_ge(*at("acc_ready", product_of(j - R1) + 1))
                    sp.dma_start(RING[j % R1], w1[l * W1N + j]).then_inc(w_landed[j % R1], 16)
                    if j < MODN // 2:
                        for i in (2 * j, 2 * j + 1):
                            if i >= RM:
                                sp.wait_ge(*at("mod_used", i - RM + 1))
                            sp.dma_start(MRING[i % RM], wmod[l * MODN + i]).then_inc(mod_landed[i % RM], 16)
            sp.wait_ge(sm["x_updated"], DEPTH * KD + START["x_updated"])
            sp.dma_start(xn_t[:, 2048:4096].rearrange("p (c t) -> p c t", c=KD), ctx_in.rearrange("c p t -> p c t")).then_inc(ctx_loaded, 16)

            def loads2(is_ctx, l):
                at2, landed2, slot2 = at2_of(is_ctx, l)
                v = view2(is_ctx)
                n, b, layer = v["L"], v["B"], 0 if is_ctx else l
                tab = tabs_c if is_ctx else tables
                if is_ctx:
                    pass
                else:
                    sp.wait_ge(*at2("x2_updated", 0))
                    sp.wait_ge(sk["kv_done"], 3)
                sp.dma_start(par2[:], p2[layer]).then_inc(sm2["loaded2"], 16)
                sp.dma_start(cs_t[:].rearrange("p (a t) -> p a t", a=2)[:, :, 0:n], rope2[:, :, 0:n] if not is_ctx else rope2[:, :, T:T + n]).then_inc(sm2["loaded2"], 16)
                sp.dma_start(big[:, 22 * n:22 * n + 512 * b], tab[6][:, 0:512 * b]).then_inc(sm2["loaded2"], 16)
                sp.dma_start(v["ZT"], tab[7][0:33, 0:n]).then_inc(sm2["loaded2"], 16)
                for i, dst in ((0, TABC), (1, TABS)):
                    sp.dma_start(dst[:, 0:b * n], tab[i][:, 0:b * n]).then_inc(sm2["tables_f"], 16)

                def weight(j, used):
                    if j >= R2:
                        sp.wait_ge(*at2(*used))
                    sp.dma_start(slot2(j), w2[layer * W2N + j]).then_inc(landed2(j)[0], 16)

                def freed(j):
                    if j < 14:
                        return "acc2", j + 1
                    if j < 14 + KD:
                        return "acc2", 20 + (j - 14) + 1
                    if j < 22 + 2 * FK:
                        return "acc2", 28 + (j - 22) + 1
                    d = j - 22 - 2 * FK
                    if d == 10:
                        return "acc2", 72 + 4
                    return "down_used", d + 1 if d < 10 else d

                for j in range(14):
                    weight(j, freed(j - R2))
                sp.wait_ge(*at2("spec_ready", b))
                for i, dst in ((2, TABC), (3, TABS)):
                    sp.dma_start(dst[:, 0:b * n], tab[i][:, 0:b * n]).then_inc(sm2["tables_h"], 16)
                for j in range(14, 14 + 4):
                    weight(j, freed(j - R2))
                sp.wait_ge(*at2("acc2", 16))
                for i, dst in ((4, TABC), (5, TABS)):
                    sp.dma_start(dst[:, 0:b * n], tab[i][:, 0:b * n]).then_inc(tables_u[0 if is_ctx else 1], 16)
                for j in range(18, W2N):
                    weight(j, freed(j - R2))

            loads2(True, 0)
            sp.wait_ge(sm2["x2_updated"], 16)
            sp.dma_start(par2[:], p2[1]).then_inc(sk["kv_loaded"], 16)
            for j in range(2):
                sp.dma_start(RING2[(W2N + j) % R2], w2[W2N + j]).then_inc(w2_landed[(W2N + j) % R2], 16)
            with sp.Fori(0, DEPTH) as l:
                loads2(False, l)
            sp.wait_ge(sm2["x2_updated"], PC["x2_updated"] + DEPTH * PX["x2_updated"])
            sp.dma_start(out.rearrange("c p t -> p c t"), x_t[:].rearrange("p (c t) -> p c t", c=KD)).then_inc(out_written, 16)
            sp.wait_ge(out_written, 16)

        @block.tensor
        def _(pe):
            for name in START:
                pe.sem_inc(sm[name], 1)
            pe.wait_ge(consts_loaded, 48)
            with pe.Fori(0, DEPTH) as l:
                def at(name, i):
                    return sm[name], l * PER1[name] + i + START.get(name, 0)

                def acc_begin(n):
                    pe.wait_ge(*at(f"acc{n % 2}_free", n // 2))
                    return ps[n % 2]

                def sums(which, sem, count, squares):
                    pe.wait_ge(*at("sum_read", which))
                    for c, (waits, s) in enumerate(squares):
                        pe.wait_ge(*at(*waits))
                        mm = pe.matmul(ps[2], ones, s, start=c == 0, stop=c == len(squares) - 1)
                    mm.then_inc(sm[sem], 1)

                def mod_product(i):
                    pe.wait_ge(mod_landed[i % RM], 16 * (l * (MODN // RM) + i // RM + 1))
                    if i == 0:
                        pe.wait_ge(small_set, 2)
                        pe.wait_ge(*at("mod_copied", 0))
                    for k in range(KD):
                        mm = pe.matmul(ps[7][:, 2 * i:2 * i + 2], MRING[i % RM][:, k * P:(k + 1) * P],
                                       cv[:, 2 * k:2 * k + 2], start=k == 0, stop=k == KD - 1)
                    mm.then_inc(sm["mod_used"], 1)

                def h_product(c, n):
                    pe.wait_ge(w_landed[c % R1], 16 * (l * (W1N // R1) + c // R1 + 1))
                    acc = acc_begin(n)
                    for k in range(KD):
                        if c == 0:
                            pe.wait_ge(*at("xn_ready", k + 1))
                        mm = pe.matmul(acc, RING[c % R1][:, k * P:(k + 1) * P], XN[k], start=k == 0, stop=k == KD - 1)
                    mm.then_inc(sm["acc_ready"], 1)
                    if c < MODN // 2:
                        mod_product(2 * c)
                        mod_product(2 * c + 1)

                sums(0, "x_summed", KD, [(("x_squared", c + 1), H[c]) for c in range(KD)])
                n = 0
                for c in range(CKV + 1):
                    h_product(c, n)
                    n += 1
                pe.wait_ge(*at("params", 32))
                acc = acc_begin(n)
                for k in range(KD):
                    mm = pe.matmul(acc[64:96, :], mw[:, k * 32:(k + 1) * 32], XN[k], start=k == 0, stop=k == KD - 1)
                mm.then_inc(sm["acc_ready"], 1)
                n += 1
                sums(1, "lat_summed", 2, [(("lat_squared", 1), SQ[0]), (("lat_squared", 2), SQ[1])])
                for c in range(DQ, BB):
                    h_product(c, n)
                    n += 1
                sums(2, "lat_summed", 1, [(("lat_squared", 3), SQ[2])])
                h_product(BB, n)
                n += 1
                h_product(BB + 1, n)
                n += 1
                for h in range(M_H):
                    acc = acc_begin(n)
                    for k in range(2):
                        pe.wait_ge(*at("lat_ready", k + 1))
                        mm = pe.matmul(acc[0:M_K, :], mw[:, 256 + k * 384 + h * M_K:256 + k * 384 + (h + 1) * M_K],
                                       H[CQ + k], start=k == 0, stop=k == 1)
                    mm.then_inc(sm["acc_ready"], 1)
                    n += 1
                for h in range(M_H):
                    acc = acc_begin(n)
                    pe.wait_ge(*at("lat_ready", 3))
                    pe.matmul(acc, mw[:, 1024 + h * P:1024 + (h + 1) * P], H[CKV],
                              start=True, stop=True).then_inc(sm["acc_ready"], 1)
                    n += 1

                def swap(i, src, waits):
                    pe.wait_ge(*waits)
                    pe.wait_ge(*at("rot_ready", i))
                    pe.sem_inc(waits_passed, 1)
                    pe.matmul(ps[6][64:96, :], cst[64:96, C_SWAP:C_SWAP + 32], src[64:96, :],
                              start=True, stop=True).then_inc(sm["swap_ready"], 1)

                swap(0, KR, at("kr_in", 1))
                for h in range(M_H):
                    swap(1 + h, QH[h], at("qc_in", h + 1))

                def values(b, n_v):
                    bank = ps[3 + b % 2]
                    if b >= 2:
                        pe.wait_ge(*at("vt_copied", b - 1))
                    pe.wait_ge(*at("acc_ready", DV + 3))
                    for i, c in enumerate((AV, DV, DV + 1)):
                        mm = pe.transpose(bank[:, i * P:(i + 1) * P], H[c][:, b * P:(b + 1) * P], ident)
                    mm.then_inc(sm["vt_ready"], 1)

                pe.wait_ge(*at("acc0_free", n // 2))
                pe.wait_ge(*at("acc1_free", n // 2))
                for b in range(NT):
                    values(b, 3)
                for b in range(NT):
                    bank = ps[3 + b % 2]
                    pe.wait_ge(*at("vt_copied", b + 3))
                    pe.wait_ge(*at("kvc_in", 4))
                    pe.sem_inc(waits_passed, 1)
                    for h in range(M_H):
                        mm = pe.transpose(bank[:, h * 64:(h + 1) * 64], VM_IN[h][64:128, b * P:(b + 1) * P], cst[64:128, C_ID + 64:C_ID + 128])
                    mm.then_inc(sm["vt_ready"], 1)

                def scores(i):
                    t = tile(i)
                    if i == 0:
                        pe.wait_ge(*at("vt_copied", 8))
                        pe.wait_ge(*at("rot_ready", 5))
                    if t["kind"] == "m":
                        pe.wait_ge(*at("kr_copied", 4))
                    if i >= 2:
                        pe.wait_ge(*at("p_exp", i - 1))
                    w = t["n"] * P
                    bank = ps[3 + i % 2]
                    pe.matmul(bank[:, 0:w], t["q"], t["k"], start=True, stop=False)
                    if t["kind"] == "a" and t["n"] == 2:
                        pe.matmul(bank[:, 0:P], ident, cst[:, C_PREV:C_PREV + P], start=False, stop=False)
                    pe.matmul(bank[:, w - P:w], ident, cst[:, C_CAUS:C_CAUS + P], start=False, stop=True).then_inc(sm["sc_ready"], 1)

                def probs_t(i):
                    t = tile(i)
                    pe.wait_ge(*at("p_norm", i + 1))
                    if i >= 1:
                        pe.wait_ge(*at("pt_copied", i))
                    for j in range(t["n"]):
                        mm = pe.transpose(ps[5][:, j * P:(j + 1) * P], pr_t[:, (i % 2) * 512 + j * P:(i % 2) * 512 + (j + 1) * P], ident)
                    mm.then_inc(sm["pt_ready"], 1)

                def values_p(i):
                    t = tile(i)
                    pe.wait_ge(*at("pt_copied", i + 1))
                    if i >= 2:
                        pe.wait_ge(*at("o_copied", i - 1))
                    c = (i % 4) * P
                    for j in range(t["n"]):
                        mm = pe.matmul(ps[6][t["base"]:t["base"] + 64, c:c + P], t["v"](t["k0"] + j),
                                       pt_t[:, (i % 2) * 512 + j * P:(i % 2) * 512 + (j + 1) * P],
                                       start=j == 0, stop=j == t["n"] - 1)
                    mm.then_inc(sm["o_ready"], 1)

                rest = list(range(BB + 2, NH))
                for s in range(TN + 3):
                    if s < TN:
                        scores(s)
                    if 0 <= s - 2 < TN:
                        probs_t(s - 2)
                    if 0 <= s - 3 < TN:
                        values_p(s - 3)
                    if s % 2 == 0 and rest:
                        c = rest.pop(0)
                        h_product(c, n)
                        n += 1
                assert not rest and n == 36

                def z_scores(u, bank, stop):
                    h, k = U[u]
                    r = slice(64 * (h % 2), 64 * (h % 2) + 64)
                    w = T - k * P
                    return pe.matmul(bank[:, 0:w], H[DK + h // 2][r, k * P:(k + 1) * P], H[DQ + h // 2][r, k * P:T],
                                     start=True, stop=stop)

                U = units()
                pe.wait_ge(*at("p_exp", TN))
                for u in range(len(U) + 1):
                    if u < len(U):
                        if u >= 2:
                            pe.wait_ge(*at("sp_done", u - 1))
                        z_scores(u, ps[3 + u % 2], True).then_inc(sm["z_ready"], 1)
                    if u >= 1:
                        h, k = U[u - 1]
                        pe.wait_ge(*at("a_exp", u - 1)) if u >= 2 else pe.wait_ge(*at("pt_copied", TN))
                        z_scores(u - 1, ps[5], False)
                        pe.wait_ge(*at("sp_masked", u))
                        for k2 in range(k, NT):
                            src = sp_t[:, (h % 2) * 1280 + OFF[k2]:(h % 2) * 1280 + OFF[k2] + T - k2 * P]
                            mm = pe.matmul(ps[5][:, (k2 - k) * P:T - k * P], ntri if k2 == k else nones, src,
                                           start=False, stop=k2 == NT - 1)
                        mm.then_inc(sm["wz_ready"], 1)
                        if k == 0:
                            base = 64 * (h % 2)
                            pe.wait_ge(*at("a_masked", u))
                            pe.wait_ge(*at("sbo_copied", h)) if h else pe.wait_ge(*at("o_copied", TN))
                            for b in range(NT):
                                for k2 in range(b + 1):
                                    mm = pe.matmul(ps[6][base:base + 64, b * P:(b + 1) * P],
                                                   vd_t[:, k2 * 256 + 64 * h:k2 * 256 + 64 * h + 64],
                                                   a_t[:, OFF[k2] + (b - k2) * P:OFF[k2] + (b - k2 + 1) * P],
                                                   start=k2 == 0, stop=k2 == b)
                            mm.then_inc(sm["sbo_ready"], 1)

                for g in range(4):
                    sums(3 + g, "y_summed", 2, [(("y_squared", 2 * g + 1), SQ[(2 * g) % 4]), (("y_squared", 2 * g + 2), SQ[(2 * g) % 4 + 1])])
                for c in range(KD):
                    j = NH + c
                    pe.wait_ge(w_landed[j % R1], 16 * (l * (W1N // R1) + j // R1 + 1))
                    acc = acc_begin(n)
                    for k in range(KD):
                        if c == 0:
                            pe.wait_ge(*at("y_ready", k + 1))
                        mm = pe.matmul(acc, RING[j % R1][:, k * P:(k + 1) * P], Y[k], start=k == 0, stop=k == KD - 1)
                    mm.then_inc(sm["acc_ready"], 1)
                    n += 1
                assert n == PER1["acc_ready"]
                sums(7, "z_summed", KD, [(("z_squared", c + 1), H[c]) for c in range(KD)])

            def run2(is_ctx, l):
                at2, landed2, slot2 = at2_of(is_ctx, l)
                v = view2(is_ctx)
                n, B, XN2, Y2, PX2, TC, TS = v["L"], v["B"], v["XN"], v["Y"], v["PX"], v["TC"], v["TS"]
                tiles = v["tiles"]

                def acc(i, w=n):
                    pe.wait_ge(*at2(f"acc2_{i % 2}_free", i // 2))
                    return ps[i % 2][:, 0:w]

                def sum_begin(which):
                    pe.wait_ge(*at2("sum2_read", which))

                def weights(i, j, rhs, waits=None):
                    pe.wait_ge(*landed2(j))
                    dst = acc(i)
                    for k in range(KD):
                        if waits:
                            pe.wait_ge(*at2(waits[0], waits[1] + k + 1))
                        mm = pe.matmul(dst, slot2(j)[:, k * P:(k + 1) * P], rhs[k], start=k == 0, stop=k == KD - 1)
                    mm.then_inc(sm2["acc2"], 1)

                def head_sum(i):
                    pe.wait_ge(*at2("hn_squared", i + 1))
                    sum_begin(1 + i)
                    pe.matmul(ps[2][:, 0:n], bd, v["SQ"][i % 4], start=True, stop=True).then_inc(sm2["hn_summed"], 1)

                def head_turn(i):
                    pe.wait_ge(*at2("hn_normed", i + 1))
                    if i == 0:
                        pe.wait_ge(*at2("flt_inv", 1))
                    else:
                        pe.wait_ge(*at2("hn_turned", i))
                    src = v["KNEW"] if i == 0 else PX2[1 + i]
                    pe.matmul(ps[3][:, 0:n], cst[:, C_SW2:C_SW2 + P], src, start=True, stop=True).then_inc(sm2["turn_ready"], 1)

                sum_begin(0)
                for c in range(KD):
                    pe.wait_ge(*at2("x2_squared", c + 1))
                    mm = pe.matmul(ps[2][:, 0:n], ones, v["H"][c], start=c == 0, stop=c == KD - 1)
                mm.then_inc(sm2["x2_summed"], 1)

                def filter_layer(i):
                    if i == 0:
                        pe.wait_ge(*at2("loaded2", 64))
                        pe.sem_inc(waits_passed, 1)
                        pe.matmul(ps[3][0:64, 0:n], par2[0:33, P_W1:P_W1 + 64], v["ZT"], start=True, stop=True).then_inc(sm2["flt_in"], 1)
                    else:
                        pe.wait_ge(*at2("flt_sin", 1))
                        pe.sem_inc(waits_passed, 1)
                        pe.matmul(ps[3][0:64, 0:n], par2[0:64, P_W2:P_W2 + 64], v["H12"], start=True, stop=True).then_inc(sm2["flt_in"], 1)

                def filter_out():
                    pe.wait_ge(*at2("flt_sin", 2))
                    for b in range(B):
                        if b >= 2:
                            pe.wait_ge(*at2("flt_decayed", b - 1))
                        pe.matmul(ps[4 + b % 2][:], v["H12"][:, b * P:(b + 1) * P], par2[0:64, P_W3:P_W3 + 512],
                                  start=True, stop=True).then_inc(sm2["flt_h"], 1)

                def filter_norm():
                    pe.wait_ge(*at2("flt_abs", 1))
                    for i in range(2):
                        for b in range(B):
                            for d in range(2):
                                mm = pe.matmul(ps[3][:, i:i + 1], v["HF"][b][:, d * 256 + i * P:d * 256 + (i + 1) * P], ones[:, 0:1],
                                               start=b + d == 0, stop=b == B - 1 and d == 1)
                    mm.then_inc(sm2["flt_norm"], 1)

                def spectrum(f):
                    pe.wait_ge(*at2("tables_f", 32))
                    pe.wait_ge(*at2("flt_sums", 1))
                    if f >= 2:
                        pe.wait_ge(*at2("spec_copied", f - 1))
                    bank = ps[6 + f % 2]
                    for b in range(B):
                        pe.matmul(bank[:, 0:256], TC[b][:, f * P:(f + 1) * P], v["HP"][b], start=b == 0, stop=b == B - 1)
                    for b in range(B):
                        mm = pe.matmul(bank[:, 256:512], TS[b][:, f * P:(f + 1) * P], v["HM"][b], start=b == 0, stop=b == B - 1)
                    mm.then_inc(sm2["spec_ready"], 1)

                def values2():
                    for b in range(B):
                        pe.wait_ge(*at2("v2_copied", b - 1)) if b >= 2 else pe.wait_ge(*at2("flt_decayed", B))
                        pe.wait_ge(*at2("acc2_0_free", 1))
                        pe.sem_inc(waits_passed, 1)
                        pe.transpose(ps[4 + b % 2][:, 0:P], PX2[0][:, b * P:(b + 1) * P], ident).then_inc(sm2["v2_ready"], 1)

                def fourier_in():
                    pe.wait_ge(*at2("acc2_0_free", 4))
                    pe.wait_ge(*at2("acc2_1_free", 4))
                    for b in range(B):
                        bank = ps[6 + b % 2]
                        pe.wait_ge(*at2("four_copied", b - 1)) if b >= 2 else pe.wait_ge(*at2("spec_copied", B))
                        for i in range(2):
                            mm = pe.matmul(bank[:, i * 256:(i + 1) * 256], PX2[6 + i][:, b * P:(b + 1) * P], cst[:, C_FD:C_FD + 256],
                                           start=True, stop=True)
                        mm.then_inc(sm2["four_ready"], 1)

                between = {0: [lambda: filter_layer(0)], 1: [lambda: filter_layer(1)], 2: [filter_out, lambda: head_sum(0)],
                           3: [filter_norm], 4: [lambda: spectrum(0), lambda: head_turn(0), lambda: head_sum(1)],
                           5: [lambda: spectrum(1), values2, lambda: head_sum(2)],
                           6: ([lambda: spectrum(2)] if B > 2 else []) + [lambda: head_turn(1), lambda: head_sum(3)],
                           7: ([lambda: spectrum(3)] if B > 2 else []) + [lambda: head_turn(2), lambda: head_sum(4)],
                           8: [lambda: head_turn(3)], 9: [lambda: head_turn(4)], 10: [fourier_in]}
                for j in range(14):
                    weights(j, j, XN2, ("xn2", 0) if j == 0 else None)
                    for step in between.get(j, []):
                        step()

                pe.wait_ge(*at2("tables_h", 32))
                pe.wait_ge(*at2("four_copied", B))
                for i in range(2):
                    dst = acc(14 + i)
                    for b in range(B):
                        pe.matmul(dst, v["FG"][b][:, i * 256:i * 256 + P], TC[b], start=b == 0, stop=False)
                        mm = pe.matmul(dst, v["FG"][b][:, i * 256 + P:(i + 1) * 256], TS[b], start=False, stop=b == B - 1)
                    mm.then_inc(sm2["acc2"], 1)
                pe.wait_ge(*at2("acc2_0_free", 8))
                pe.wait_ge(*at2("acc2_1_free", 8))
                for i in range(2):
                    dst = acc(16 + i)
                    for k in range(2):
                        mm = pe.matmul(dst, par2[:, NP2 + k * 256 + i * P:NP2 + k * 256 + (i + 1) * P], PX2[6 + k], start=k == 0, stop=k == 1)
                    mm.then_inc(sm2["acc2"], 1)

                KB = v["W"] // P

                def scores(i):
                    b, j, half = tiles[i]
                    r = slice(64 * half, 64 * half + 64)
                    if i == 0:
                        pe.wait_ge(*at2("hn_turned", 5))
                        pe.wait_ge(*at2("v2_copied", B))
                        pe.wait_ge(*at2("md_ready", 1))
                    if i >= 2:
                        pe.wait_ge(*at2("pe2", i - 1))
                    if i == 1:
                        pe.wait_ge(*at2("four_copied", B))
                    o = 1536 + 1024 * (i % 2)
                    for c0 in range(0, v["W"], 512):
                        c1 = min(c0 + 512, v["W"])
                        mm = pe.matmul(ps_t[:, o + c0:o + c1], PX2[2 + j][r, b * P:(b + 1) * P], v["K"][r, c0:c1], start=True, stop=True)
                    mm.then_inc(sm2["sc2"], 1)

                def probs_t(i):
                    pe.wait_ge(*at2("pn2", i + 1))
                    if i >= 1:
                        pe.wait_ge(*at2("pc2", i))
                        if KB > 4:
                            pe.wait_ge(*at2("pd2", i))
                    else:
                        sum_begin(6)
                    for k in range(KB):
                        bank = ps[7][:, k * P:(k + 1) * P] if k < 4 else ps[2][:, (k - 4) * P:(k - 3) * P]
                        mm = pe.transpose(bank, v["PR"][i % 2][:, k * P:(k + 1) * P], ident)
                    mm.then_inc(sm2["pt2"], 1)

                def values_p(i):
                    b, j, half = tiles[i]
                    pe.wait_ge(*at2("pc2", i + 1))
                    if KB > 4:
                        pe.wait_ge(*at2("pd2", i + 1))
                    pe.wait_ge(*at2("oc2", i - 1)) if i >= 2 else pe.wait_ge(*at2("acc2_0_free", 9))
                    r = slice(64 * half, 64 * half + 64)
                    for k in range(KB):
                        mm = pe.matmul(ps[0][r, 0:P], v["V"][k][:, r], v["PT"][i % 2][:, k * P:(k + 1) * P], start=k == 0, stop=k == KB - 1)
                    mm.then_inc(sm2["o2"], 1)

                for i in range(len(tiles) + 3):
                    if i < len(tiles):
                        scores(i)
                    if 0 <= i - 2 < len(tiles):
                        probs_t(i - 2)
                    if 0 <= i - 3 < len(tiles):
                        values_p(i - 3)

                pe.wait_ge(*at2("u_ready", 2))
                for b in range(B):
                    bank = ps[3 + b % 2]
                    pe.wait_ge(*at2("ut_copied", b - 1)) if b >= 2 else pe.wait_ge(*at2("pe2", len(tiles)))
                    for i in range(2):
                        mm = pe.transpose(bank[:, i * P:(i + 1) * P], v["UC"][2 + i][:, b * P:(b + 1) * P], ident)
                    mm.then_inc(sm2["ut_ready"], 1)
                pe.wait_ge(tables_u[0 if is_ctx else 1], 32 if is_ctx else l * 32 + 32)
                pe.wait_ge(*at2("ut_copied", B))
                for f in range(B):
                    bank = ps[5 + f % 2]
                    if f >= 2:
                        pe.wait_ge(*at2("us_mul", f - 1))
                    for b in range(B):
                        pe.matmul(bank[:, 0:256], TC[b][:, f * P:(f + 1) * P], v["UT"][b], start=b == 0, stop=b == B - 1)
                    for b in range(B):
                        mm = pe.matmul(bank[:, 256:512], TS[b][:, f * P:(f + 1) * P], v["UT"][b], start=b == 0, stop=b == B - 1)
                    mm.then_inc(sm2["us_ready"], 1)
                pe.wait_ge(*at2("oc2", len(tiles)))
                for i in range(2):
                    dst = acc(18 + i)
                    for f in range(B):
                        pe.wait_ge(*at2("us_done", f + 1))
                        pe.matmul(dst, v["YR"][f][:, i * P:(i + 1) * P], TC[f], start=f == 0, stop=False)
                        mm = pe.matmul(dst, v["YI"][f][:, i * P:(i + 1) * P], TS[f], start=False, stop=f == B - 1)
                    mm.then_inc(sm2["acc2"], 1)

                pe.wait_ge(*at2("hy_out", 2))
                for c in range(KD):
                    weights(20 + c, 14 + c, Y2)

                def z_sum(which, r):
                    sum_begin(r)
                    for c in range(KD):
                        pe.wait_ge(*at2("z2_squared", 8 * which + c + 1))
                        mm = pe.matmul(ps[2][:, 0:n], ones, (v["H"] if which == 0 else Y2)[c], start=c == 0, stop=c == KD - 1)
                    mm.then_inc(sm2["z2_summed"], 1)

                z_sum(0, 6)
                sum_begin(7)
                for c in range(KD):
                    pe.wait_ge(*at2("x2_squared", 8 + c + 1))
                    mm = pe.matmul(ps[2][:, 0:n], ones, v["H"][c], start=c == 0, stop=c == KD - 1)
                mm.then_inc(sm2["x2_summed"], 1)
                pe.wait_ge(*at2("xn2", 16))
                pe.sem_inc(waits_passed, 1)
                with pe.Fori(0, FK // 2) as g:
                    for q in range(4):
                        sem, val = landed2(22 + q)
                        pe.wait_ge(sem, g * 16 + val)
                        i = 28 + q
                        sem, val = at2(f"acc2_{i % 2}_free", i // 2)
                        pe.wait_ge(sem, g * 2 + val)
                        for k in range(KD):
                            mm = pe.matmul(ps[i % 2][:, 0:n], slot2(22 + q)[:, k * P:(k + 1) * P], XN2[k], start=k == 0, stop=k == KD - 1)
                        mm.then_inc(sm2["acc2"], 1)
                for c in range(KD):
                    dst = acc(72 + c)
                    for k in range(FK):
                        t = c * FK + k
                        if t % 8 == 0:
                            pe.wait_ge(*landed2(22 + 2 * FK + t // 8))
                        if c == 0:
                            pe.wait_ge(*at2("g_ready", k + 1))
                        mm = pe.matmul(dst, slot2(22 + 2 * FK + t // 8)[:, (t % 8) * P:(t % 8 + 1) * P], v["G"][k], start=k == 0, stop=k == FK - 1)
                        if t % 8 == 7 and k < FK - 1:
                            mm.then_inc(sm2["down_used"], 1)
                    mm.then_inc(sm2["acc2"], 1)
                z_sum(1, 8)

            run2(True, 0)
            v = view2(True)
            for c in range(KD):
                pe.wait_ge(sk["kv_squared"], c + 1)
                mm = pe.matmul(ps[2][:, 0:LC], ones, v["H"][c], start=c == 0, stop=c == KD - 1)
            mm.then_inc(sk["kv_summed"], 1)
            for j in range(2):
                pe.wait_ge(w2_landed[(W2N + j) % R2], 16 * ((W2N + j) // R2 + 1))
                for k in range(KD):
                    pe.wait_ge(sk["kv_xn"], k + 1)
                    mm = pe.matmul(ps[j][:, 0:LC], RING2[(W2N + j) % R2][:, k * P:(k + 1) * P], v["XN"][k], start=k == 0, stop=k == KD - 1)
                mm.then_inc(sk["kv_acc"], 1)
            pe.wait_ge(sk["kv_ksq"], 1)
            pe.matmul(ps[2][:, 0:LC], bd, v["SQ"][0], start=True, stop=True).then_inc(sk["kv_ksum"], 1)
            pe.wait_ge(sk["kv_taken"], 1)
            for b in range(2):
                mm = pe.transpose(ps[3][:, b * P:(b + 1) * P], v["PX"][0][:, b * P:(b + 1) * P], ident)
            mm.then_inc(sk["kv_tr"], 1)
            with pe.Fori(0, DEPTH) as l:
                run2(False, l)

        @block.scalar
        def _(act):
            act.wait_ge(consts_loaded, 48)
            for i, dst in ((0, SIN), (1, COS)):
                act.wait_ge(sin_in, i + 1)
                nc.scalar.activation(dst, dst, ACT.Sin).then_inc(rope_ready, 1)
            nc.scalar.activation(cv[:, 16:32], modp_t[:, DEPTH * 96:DEPTH * 96 + 16], ACT.Sigmoid).then_inc(small_set, 1)
            act.wait_ge(x_loaded, 16)
            with act.Fori(0, DEPTH) as l:
                def at(name, i):
                    return sm[name], l * PER1[name] + i + START.get(name, 0)

                link = Link(act, sm["link_act"], l * PER1["link_act"])
                nc.scalar.preload_act_table_set(LNEXP)

                def rstd(which, sem, i, width, dst):
                    act.wait_ge(*at(sem, i))
                    nc.scalar.activation(dst, ps[2], ACT.Ln, bias=eps, scale=1.0 / width).then_inc(sm["sum_read"], 1)
                    act.wait_ge(*at("sum_read", which + 1))
                    nc.scalar.activation(dst, dst, ACT.Exp, scale=-0.5).then_inc(sm["rstd_ready"], 1)

                for c in range(KD):
                    act.wait_ge(*at("x_updated", 0))
                    nc.scalar.activation(H[c], X[c], ACT.Square).then_inc(sm["x_squared"], 1)
                rstd(0, "x_summed", 1, D, RSTD[0])

                def take(n, dst, scale=1.0, rows=slice(0, P), extra=None):
                    act.wait_ge(*at("acc_ready", n + 1))
                    nc.scalar.activation(dst, ps[n % 2][rows, :], ACT.Copy, scale=scale).then_inc(sm[f"acc{n % 2}_free"], 1)

                take(0, H[AQ], A_D ** -0.5)
                take(2, H[AK])
                take(4, H[CQ])
                act.wait_ge(*at("acc0_free", 3))
                nc.scalar.activation(SQ[0], H[CQ], ACT.Square).then_inc(sm["lat_squared"], 1)
                act.wait_ge(*at("acc1_free", 3))
                nc.scalar.activation(SQ[1], H[CQ + 1], ACT.Square).then_inc(sm["lat_squared"], 1)
                take(6, H[CKV])
                act.wait_ge(*at("acc0_free", 4))
                nc.scalar.activation(SQ[2], H[CKV], ACT.Square).then_inc(sm["lat_squared"], 1)
                rstd(1, "lat_summed", 1, 256, RSTD[1])
                take(8, H[DQ], 0.125)
                take(10, H[DK])
                take(12, H[DV])
                act.wait_ge(*at("lat_ready", 2))
                rstd(2, "lat_summed", 2, 128, RSTD[1])
                take(14, H[BB])
                for h in range(M_H):
                    act.wait_ge(*at("acc_ready", 17 + h))
                    nc.scalar.activation(QH[h][0:M_K, :], ps[h % 2][0:M_K, :], ACT.Copy).then_inc(sm["qc_in"], 1)
                    act.wait_ge(*at("qc_in", h + 1))
                    act.sem_inc(sm[f"acc{h % 2}_free"], 1)
                for h in range(M_H):
                    act.wait_ge(*at("acc_ready", 21 + h))
                    nc.scalar.activation(KH[h][0:64, :], ps[h % 2][0:64, :], ACT.Copy)
                    nc.scalar.activation(VM_IN[h][64:128, :], ps[h % 2][64:128, :], ACT.Copy).then_inc(sm["kvc_in"], 1)
                    act.wait_ge(*at("kvc_in", h + 1))
                    act.sem_inc(sm[f"acc{h % 2}_free"], 1)
                act.wait_ge(*at("rot_ready", 1))
                for h in range(M_H):
                    nc.scalar.activation(KH[h][64:96, :], KR[64:96, :], ACT.Copy).then_inc(sm["kr_copied"], 1)

                rest = list(range(BB + 2, NH))
                n = 24
                for s in range(TN + 3):
                    if s < TN:
                        t = tile(s)
                        w = t["n"] * P
                        act.wait_ge(*at("negmax", s + 1))
                        if s >= 2:
                            act.wait_ge(*at("pt_ready", s - 1))
                        nc.scalar.activation(pr_t[:, (s % 2) * 512:(s % 2) * 512 + w], ps[3 + s % 2][:, 0:w], ACT.Exp,
                                             bias=st_t[:, 32 + s:33 + s], scale=1.0 if t["kind"] == "a" else M_SCALE,
                                             accum_out=st_t[:, 64 + s:65 + s]).then_inc(sm["p_exp"], 1)
                        if t["kind"] == "a":
                            link(nc.scalar.activation(st_t[:, 128 + s:129 + s], pcol(P_SINK + t["h"]), ACT.Exp,
                                                      bias=st_t[:, 32 + s:33 + s]))
                    if 0 <= s - 2 < TN:
                        i = s - 2
                        w = tile(i)["n"] * P
                        act.wait_ge(*at("pt_ready", i + 1))
                        if i >= 2:
                            act.wait_ge(*at("o_ready", i - 1))
                        nc.scalar.activation(pt_t[:, (i % 2) * 512:(i % 2) * 512 + w], ps[5][:, 0:w], ACT.Copy).then_inc(sm["pt_copied"], 1)
                    if s % 2 == 0 and rest:
                        c = rest.pop(0)
                        if n % 2 == 0:
                            take(n, H[c])
                        n += 1

                U = units()
                for u in range(len(U) + 1):
                    if u < len(U):
                        w = T - U[u][1] * P
                        lz = LZ[u % 2][:, 0:w]
                        act.wait_ge(*at("z_ready", u + 1))
                        if u >= 2:
                            act.wait_ge(*at("sp_done", u - 1))
                        link(nc.scalar.activation(lz, ps[3 + u % 2][:, 0:w], ACT.Abs))
                        link(nc.scalar.activation(lz, lz, ACT.Exp, scale=-1.0))
                        nc.scalar.activation(lz, lz, ACT.Ln, bias=one).then_inc(sm["z_ln"], 1)
                    if u >= 1:
                        h, k = U[u - 1]
                        w = T - k * P
                        act.wait_ge(*at("wz_ready", u))
                        if k == NT - 1 and h:
                            act.wait_ge(*at("sbo_ready", h))
                        nc.scalar.activation(a_t[:, OFF[k]:OFF[k] + w], ps[5][:, 0:w], ACT.Exp).then_inc(sm["a_exp"], 1)

                def group(g):
                    for i in range(2):
                        c = 2 * g + i
                        if g in (0, 2):
                            act.wait_ge(*at("o_copied", TN))
                        elif g == 1:
                            act.wait_ge(*at("conv_done", 2))
                        else:
                            act.wait_ge(*at("sbo_copied", 4))
                        if g >= 2:
                            act.wait_ge(*at("y_summed", g - 1))
                        nc.scalar.activation(SQ[c % 4], Y[c], ACT.Square).then_inc(sm["y_squared"], 1)
                    if g >= 2:
                        act.wait_ge(*at("y_normed", 2 * g - 2))
                    rstd(3 + g, "y_summed", g + 1, 256, RSTD[g % 2])

                for g in range(4):
                    group(g)
                act.wait_ge(*at("acc0_free", 18))
                act.wait_ge(*at("acc1_free", 18))
                for c in range(KD):
                    nc.scalar.activation(H[BB + c - 13 + 0], H[GATE + c], ACT.Sigmoid).then_inc(sm["gate_sig"], 1)
                nc.scalar.preload_act_table_set(LNEXP)
                for c in range(KD):
                    n = 36 + c
                    act.wait_ge(*at("acc_ready", n + 1))
                    act.wait_ge(*at("y_ready", KD))
                    nc.scalar.activation(H[c], ps[n % 2], ACT.Square).then_inc(sm["z_squared"], 1)
                rstd(7, "z_summed", 1, D, RSTD[0])
                assert link.n == PER1["link_act"]

            def run2(is_ctx, l):
                at2, landed2, slot2 = at2_of(is_ctx, l)
                v = view2(is_ctx)
                n, B, tiles, per = v["L"], v["B"], v["tiles"], PC if is_ctx else PX

                def rstd(which, sem, i, width, dst):
                    act.wait_ge(*at2(sem, i))
                    nc.scalar.activation(dst, ps[2][:, 0:n], ACT.Ln, bias=eps, scale=1.0 / width).then_inc(sm2["sum2_read"], 1)
                    act.wait_ge(*at2("sum2_read", which + 1))
                    nc.scalar.activation(dst, dst, ACT.Exp, scale=-0.5).then_inc(sm2["rstd2"], 1)

                def take(i, dst):
                    act.wait_ge(*at2("acc2", i + 1))
                    nc.scalar.activation(dst, ps[i % 2][:, 0:n], ACT.Copy).then_inc(sm2[f"acc2_{i % 2}_free"], 1)

                def pre_norm(which, r, shift):
                    for c in range(KD):
                        nc.scalar.activation(v["H"][c], v["X"][c], ACT.Square).then_inc(sm2["x2_squared"], 1)
                    rstd(r, "x2_summed", which + 1, D, v["RSTD"][0])
                    for c in range(KD):
                        act.wait_ge(*at2("xs2", 8 * which + c + 1))
                        nc.scalar.activation(v["XN"][c], v["XN"][c], ACT.Identity, bias=md[:, shift + c:shift + c + 1]).then_inc(sm2["xn2"], 1)

                nc.scalar.preload_act_table_set(LNEXP)
                act.wait_ge(*at2("x2_updated", 0))
                if not is_ctx:
                    act.wait_ge(sk["kv_done"], 3)
                pre_norm(0, 0, SH1)

                def head_square(i):
                    if i == 4:
                        act.wait_ge(*at2("hn_summed", 1))
                    act.wait_ge(*at2(f"acc2_{(1 + i) % 2}_free", (1 + i) // 2 + 1))
                    nc.scalar.activation(v["SQ"][i % 4], v["PX"][1 + i], ACT.Square).then_inc(sm2["hn_squared"], 1)

                def head_rstd(i):
                    if i >= 2:
                        act.wait_ge(*at2("hn_normed", i - 1))
                    elif i == 0:
                        act.wait_ge(*at2("xs2", 8))
                    rstd(1 + i, "hn_summed", i + 1, 64, v["RSTD"][i % 2])

                def filter_sin(i):
                    act.wait_ge(*at2("flt_arg", i + 1))
                    nc.scalar.activation(v["H12"], v["H12"], ACT.Sin).then_inc(sm2["flt_sin"], 1)

                def filter_abs():
                    act.wait_ge(*at2("flt_sums", 1))
                    nc.scalar.activation(big[:, 14 * n:14 * n + 512 * B], big[:, 14 * n:14 * n + 512 * B], ACT.Abs).then_inc(sm2["flt_abs"], 1)

                def spec_copy(f):
                    act.wait_ge(*at2("spec_ready", f + 1))
                    nc.scalar.activation(v["SPEC"][f], ps[6 + f % 2][:], ACT.Copy).then_inc(sm2["spec_copied"], 1)

                def conv_mid(i, c, dst):
                    act.wait_ge(*at2("acc2", i + 1))
                    nc.scalar.activation(dst, ps[i % 2][:, 0:n], ACT.Identity, bias=p2c(P_HCB + c), scale=p2c(P_HCW + 6 + c)).then_inc(sm2["conv_mid"], 1)

                between = {0: [lambda: filter_sin(0)], 1: [lambda: filter_sin(1), lambda: nc.scalar.preload_act_table_set(LNEXP), lambda: head_square(0)],
                           2: [lambda: head_square(1), filter_abs, lambda: head_rstd(0)], 3: [lambda: head_square(2)],
                           4: [lambda: spec_copy(0), lambda: head_square(3), lambda: head_rstd(1)],
                           5: [lambda: spec_copy(1), lambda: head_square(4), lambda: head_rstd(2)],
                           6: ([lambda: spec_copy(2)] if B > 2 else []) + [lambda: head_rstd(3)],
                           7: ([lambda: spec_copy(3)] if B > 2 else []) + [lambda: head_rstd(4)]}
                for j in range(14):
                    if j in (0, 2, 4, 6):
                        take(j, v["PX"][j])
                    if j >= 8:
                        conv_mid(j, j - 8, v["UC"][j - 8])
                    for step in between.get(j, []):
                        step()
                act.wait_ge(*at2("four_copied", B))
                take(14, v["PX"][6])
                take(16, v["Y"][4])

                for i in range(len(tiles) + 2):
                    if i < len(tiles):
                        act.wait_ge(*at2("neg2", i + 1))
                        if i >= 2:
                            act.wait_ge(*at2("pt2", i - 1))
                        nc.scalar.activation(v["PR"][i % 2][:, 0:v["W"]], ps_t[:, 1536 + 1024 * (i % 2):1536 + 1024 * (i % 2) + v["W"]], ACT.Exp,
                                             bias=st_t[:, 32 + i:33 + i], scale=0.125, accum_out=st_t[:, 64 + i:65 + i]).then_inc(sm2["pe2"], 1)
                    if i >= 2:
                        t = i - 2
                        act.wait_ge(*at2("pt2", t + 1))
                        if t >= 2:
                            act.wait_ge(*at2("o2", t - 1))
                        w = min(512, v["W"])
                        nc.scalar.activation(v["PT"][t % 2][:, 0:w], ps[7][:, 0:w], ACT.Copy).then_inc(sm2["pc2"], 1)

                def z_square(which, i0, dst):
                    for c in range(KD):
                        i = i0 + c
                        act.wait_ge(*at2("acc2", i + 1))
                        nc.scalar.activation(dst[c], ps[i % 2][:, 0:n], ACT.Square).then_inc(sm2["z2_squared"], 1)

                z_square(0, 20, v["H"])
                rstd(6, "z2_summed", 1, D, v["RSTD"][0])
                act.wait_ge(*at2("zn2", 8))
                act.wait_ge(*at2("x2_updated", 8))
                pre_norm(1, 7, SH2)
                with act.Fori(0, FK // 2) as g:
                    for q in range(4):
                        i = 28 + q
                        dst = (v["AG"] if q % 2 == 0 else v["AV"])[q // 2]
                        c = g * 2 + q // 2 + FK * (q % 2)
                        sem, val = at2("acc2", i + 1)
                        act.wait_ge(sem, g * 4 + val)
                        sem, val = at2("g_ready", q // 2 - 2 + FSTART)
                        act.wait_ge(sem, g * 2 + val)
                        nc.scalar.activation(dst, ps[i % 2][:, 0:n], ACT.Identity, bias=par2[:, bass.ds(P_FCB + c, 1)],
                                             scale=par2[:, bass.ds(P_FCW + 2 * FK + c, 1)]).then_inc(sm2["conv_mid"], 1)
                        if q % 2 == 1:
                            sem, val = at2("conv2", 6 + q)
                            act.wait_ge(sem, g * 4 + val)
                            nc.scalar.activation(v["SG"][q // 2], v["AG"][q // 2], ACT.Sigmoid).then_inc(sm2["gate_sig2"], 1)
                nc.scalar.preload_act_table_set(LNEXP)
                z_square(1, 72, v["Y"])
                rstd(8, "z2_summed", 2, D, v["RSTD"][0])

            act.wait_ge(ctx_loaded, 16)
            run2(True, 0)
            v = view2(True)
            act.wait_ge(sm2["x2_updated"], 16)
            for c in range(KD):
                nc.scalar.activation(v["H"][c], v["X"][c], ACT.Square).then_inc(sk["kv_squared"], 1)
            act.wait_ge(sk["kv_summed"], 1)
            nc.scalar.activation(v["RSTD"][0], ps[2][:, 0:LC], ACT.Ln, bias=eps, scale=1.0 / D).then_inc(sk["kv_link"], 1)
            act.wait_ge(sk["kv_link"], 1)
            nc.scalar.activation(v["RSTD"][0], v["RSTD"][0], ACT.Exp, scale=-0.5).then_inc(sk["kv_rstd"], 1)
            for c in range(KD):
                act.wait_ge(sk["kv_xs"], c + 1)
                nc.scalar.activation(v["XN"][c], v["XN"][c], ACT.Identity, bias=md[:, SH1 + c:SH1 + c + 1]).then_inc(sk["kv_xn"], 1)
            act.wait_ge(sk["kv_acc"], 1)
            nc.scalar.activation(v["PX"][0], ps[0][:, 0:LC], ACT.Copy).then_inc(sk["kv_taken"], 1)
            act.wait_ge(sk["kv_acc"], 2)
            nc.scalar.activation(v["SQ"][0], ps[1][:, 0:LC], ACT.Square).then_inc(sk["kv_ksq"], 1)
            act.wait_ge(sk["kv_ksum"], 1)
            nc.scalar.activation(v["RSTD"][1], ps[2][:, 0:LC], ACT.Ln, bias=eps, scale=1.0 / 64).then_inc(sk["kv_link"], 1)
            act.wait_ge(sk["kv_link"], 2)
            nc.scalar.activation(v["RSTD"][1], v["RSTD"][1], ACT.Exp, scale=-0.5).then_inc(sk["kv_krstd"], 1)
            with act.Fori(0, DEPTH) as l:
                run2(False, l)

        @block.vector
        def _(dve):
            nc.vector.memset(eps_t[:, 0:1], EPS)
            nc.vector.memset(eps_t[:, 1:2], 1.0).then_inc(small_set, 1)
            dve.wait_ge(consts_loaded, 48)
            link = Link(dve, link_rope, 0)
            ang = ROT[0][64:96, :]
            kk = ROT[1][64:96, :]
            link(nc.vector.tensor_copy(ang, pos_t[64:96, :]))
            link(nc.vector.tensor_scalar(ang, ang, cst[64:96, C_FREQ:C_FREQ + 1], None, ALU.mult))
            for dst, quarter in ((SIN, 0.0), (COS, 0.25)):
                link(nc.vector.tensor_scalar(kk, ang, INV_2PI, quarter, ALU.mult, ALU.add))
                link(nc.vector.tensor_scalar(kk, kk, MAGIC, None, ALU.add))
                link(nc.vector.tensor_scalar(kk, kk, -MAGIC, None, ALU.add))
                link(nc.vector.scalar_tensor_tensor(dst, kk, -TP_A, ang, ALU.mult, ALU.add))
                link(nc.vector.scalar_tensor_tensor(dst, kk, -TP_B, dst, ALU.mult, ALU.add))
                link(nc.vector.scalar_tensor_tensor(dst, kk, -TP_C, dst, ALU.mult, ALU.add))
                if quarter:
                    link(nc.vector.tensor_scalar(dst, dst, HALF_PI, None, ALU.add))
                nc.vector.tensor_scalar(dst, dst, PI, -PI, ALU.min, ALU.max).then_inc(sin_in, 1)
            dve.wait_ge(small_set, 2)
            nc.vector.tensor_tensor(cv[:, 0:16], cv[:, 16:32], modp_t[:, DEPTH * 96:DEPTH * 96 + 16], ALU.mult).then_inc(small_set, 1)
            dve.wait_ge(rope_ready, 2)
            dve.wait_ge(x_loaded, 16)
            with dve.Fori(0, DEPTH) as l:
                def at(name, i):
                    return sm[name], l * PER1[name] + i + START.get(name, 0)

                link = Link(dve, sm["link_dve"], l * PER1["link_dve"])
                dve.wait_ge(*at("params", 32))
                dve.wait_ge(*at("rstd_ready", 1))
                for c in range(KD):
                    nc.vector.scalar_tensor_tensor(XN[c], X[c], pcol(P_PRE + c), RSTD[0], ALU.mult, ALU.mult).then_inc(sm["xn_ready"], 1)

                def take(n, dst, scale=None):
                    dve.wait_ge(*at("acc_ready", n + 1))
                    if scale is None:
                        ins = nc.vector.tensor_copy(dst, ps[n % 2])
                    else:
                        ins = nc.vector.tensor_scalar(dst, ps[n % 2], scale, None, ALU.mult)
                    ins.then_inc(sm[f"acc{n % 2}_free"], 1)

                take(1, H[AQ + 1], A_D ** -0.5)
                take(3, H[AV])
                take(5, H[CQ + 1])
                dve.wait_ge(*at("acc_ready", 8))
                nc.vector.tensor_copy(KR[64:96, :], ps[1][64:96, :]).then_inc(sm["kr_in"], 1)
                dve.wait_ge(*at("kr_in", 1))
                dve.sem_inc(sm["acc1_free"], 1)
                take(9, H[DQ + 1], 0.125)
                dve.wait_ge(*at("rstd_ready", 2))
                dve.wait_ge(*at("lat_squared", 2))
                for k in range(2):
                    nc.vector.scalar_tensor_tensor(H[CQ + k], H[CQ + k], pcol(P_GCQ + k), RSTD[1], ALU.mult, ALU.mult).then_inc(sm["lat_ready"], 1)
                take(11, H[DK + 1])
                take(13, H[DV + 1])
                dve.wait_ge(*at("rstd_ready", 3))
                nc.vector.scalar_tensor_tensor(H[CKV], H[CKV], pcol(P_GCKV), RSTD[1], ALU.mult, ALU.mult).then_inc(sm["lat_ready"], 1)
                take(15, H[BB + 1])

                def rotate(i, dst):
                    dve.wait_ge(*at("swap_ready", i + 1))
                    nc.vector.tensor_tensor(ROT[0][64:96, :], ps[6][64:96, :], SIN, ALU.mult)
                    link(nc.vector.tensor_tensor(dst, dst, COS, ALU.mult))
                    nc.vector.tensor_tensor(dst, dst, ROT[0][64:96, :], ALU.add).then_inc(sm["rot_ready"], 1)
                    dve.wait_ge(*at("rot_ready", i + 1))

                rotate(0, KR[64:96, :])
                for h in range(M_H):
                    rotate(1 + h, QH[h][64:96, :])
                for b in range(NT):
                    dve.wait_ge(*at("vt_ready", b + 1))
                    nc.vector.tensor_copy(va_t[:, b * P:(b + 1) * P], ps[3 + b % 2][:, 0:P])
                    nc.vector.tensor_copy(vd_t[:, b * 256:(b + 1) * 256], ps[3 + b % 2][:, P:3 * P]).then_inc(sm["vt_copied"], 1)
                for b in range(NT):
                    dve.wait_ge(*at("vt_ready", NT + b + 1))
                    nc.vector.tensor_copy(vm_t[:, b * 256:(b + 1) * 256], ps[3 + b % 2][:, 0:256]).then_inc(sm["vt_copied"], 1)

                rest = list(range(BB + 2, NH))
                n = 24
                for s in range(TN + 4):
                    if s < TN:
                        t = tile(s)
                        w = t["n"] * P
                        mx, neg = st_t[:, s:s + 1], st_t[:, 32 + s:33 + s]
                        dve.wait_ge(*at("sc_ready", s + 1))
                        link(nc.vector.tensor_reduce(mx, ps[3 + s % 2][:, 0:w], AX_X, ALU.max))
                        if t["kind"] == "a":
                            nc.vector.tensor_scalar(neg, mx, pcol(P_SINK + t["h"]), -1.0, ALU.max, ALU.mult).then_inc(sm["negmax"], 1)
                        else:
                            nc.vector.tensor_scalar(neg, mx, -M_SCALE, None, ALU.mult).then_inc(sm["negmax"], 1)
                    if 0 <= s - 1 < TN:
                        i = s - 1
                        t = tile(i)
                        w = t["n"] * P
                        den = st_t[:, 64 + i:65 + i]
                        inv = st_t[:, 96 + i:97 + i]
                        dve.wait_ge(*at("p_exp", i + 1))
                        if t["kind"] == "a":
                            dve.wait_ge(sm["link_act"], l * PER1["link_act"] + i + 1)
                            link(nc.vector.tensor_tensor(den, den, st_t[:, 128 + i:129 + i], ALU.add))
                        link(nc.vector.reciprocal(inv, den))
                        pr = pr_t[:, (i % 2) * 512:(i % 2) * 512 + w]
                        nc.vector.tensor_scalar(pr, pr, inv, None, ALU.mult).then_inc(sm["p_norm"], 1)
                    if 0 <= s - 3 < TN:
                        i = s - 3
                        t = tile(i)
                        dve.wait_ge(*at("o_ready", i + 1))
                        nc.vector.tensor_copy(t["y"][t["base"]:t["base"] + 64, t["b"] * P:(t["b"] + 1) * P],
                                              ps[6][t["base"]:t["base"] + 64, (i % 4) * P:(i % 4 + 1) * P]).then_inc(sm["o_copied"], 1)
                    if s % 2 == 0 and rest:
                        c = rest.pop(0)
                        if n % 2 == 1:
                            take(n, H[c])
                        n += 1
                        if c == BX + 1:
                            for i in range(2):
                                dve.wait_ge(*at("acc0_free", (24 + 4) // 2))
                                u, y = H[BC + i], Y[2 + i]
                                w = [pcol(P_CW + 2 * k + i) for k in range(3)]
                                dve.wait_ge(*at("acc1_free", n // 2))
                                dve.wait_ge(*at("acc0_free", n // 2))
                                link(nc.vector.tensor_tensor(u, u, H[BX + i], ALU.mult))
                                link(nc.vector.tensor_scalar(y, u, w[2], pcol(P_CB + i), ALU.mult, ALU.add))
                                link(nc.vector.scalar_tensor_tensor(y[:, 1:T], u[:, 0:T - 1], w[1], y[:, 1:T], ALU.mult, ALU.add))
                                link(nc.vector.scalar_tensor_tensor(y[:, 2:T], u[:, 0:T - 2], w[0], y[:, 2:T], ALU.mult, ALU.add))
                                nc.vector.tensor_tensor(y, y, H[BB + i], ALU.mult).then_inc(sm["conv_done"], 1)

                U = units()
                for u in range(len(U) + 1):
                    if u < len(U):
                        h, k = U[u]
                        w = T - k * P
                        dve.wait_ge(*at("z_ln", u + 1))
                        if k == NT - 1 and h >= 2:
                            dve.wait_ge(*at("wz_ready", 4 * (h - 1)))
                        nc.vector.scalar_tensor_tensor(sp_t[:, (h % 2) * 1280 + OFF[k]:(h % 2) * 1280 + OFF[k] + w],
                                                       ps[3 + u % 2][:, 0:w], 0.0, LZ[u % 2][:, 0:w], ALU.max, ALU.add).then_inc(sm["sp_done"], 1)
                    if u >= 1 and U[u - 1][1] == 0:
                        h = U[u - 1][0]
                        base = 64 * (h % 2)
                        dve.wait_ge(*at("sbo_ready", h + 1))
                        nc.vector.tensor_copy(Y[6 + h // 2][base:base + 64, :], ps[6][base:base + 64, :]).then_inc(sm["sbo_copied"], 1)

                for g in range(4):
                    dve.wait_ge(*at("rstd_ready", 4 + g))
                    for c in (2 * g, 2 * g + 1):
                        dve.wait_ge(*at("y_squared", c + 1))
                        nc.vector.scalar_tensor_tensor(Y[c], Y[c], pcol(P_GRP + c), RSTD[g % 2], ALU.mult, ALU.mult).then_inc(sm["y_normed"], 1)
                for c in range(KD):
                    dve.wait_ge(*at("gate_mul", c + 1))
                    dve.wait_ge(*at("y_normed", c + 1))
                    nc.vector.tensor_tensor(Y[c], Y[c], H[GATE + c], ALU.mult).then_inc(sm["y_ready"], 1)
                for c in range(KD):
                    n = 36 + c
                    dve.wait_ge(*at("z_squared", c + 1))
                    nc.vector.tensor_copy(Z[c], ps[n % 2]).then_inc(sm[f"acc{n % 2}_free"], 1)
                dve.wait_ge(*at("rstd_ready", 8))
                dve.wait_ge(*at("acc0_free", 22))
                dve.wait_ge(*at("acc1_free", 22))
                for c in range(KD):
                    nc.vector.scalar_tensor_tensor(Z[c], Z[c], pcol(P_POST + c), RSTD[0], ALU.mult, ALU.mult).then_inc(sm["zn_ready"], 1)
                dve.wait_ge(*at("mod_used", MODN))
                nc.vector.tensor_tensor(mods[:, bass.ds(l * 96, 96)], ps[7][:, 0:96], modp_t[:, bass.ds(l * 96, 96)], ALU.add).then_inc(sm["mod_copied"], 1)
                assert link.n == PER1["link_dve"]

            def gains(layer, which, link):
                link(nc.vector.tensor_copy(md[:, 0:48], mods[:, bass.ds(layer * 96, 96)].rearrange("p (c w) -> p c w", w=2)[:, :, which]))
                for dst, gain, mod, plus in ((G1, P_GPM, SC1, 1.0), (GA1, P_GPOM, GT1, 0.0), (G2, P_GPF, SC2, 1.0), (GA2, P_GPOF, GT2, 0.0)):
                    ins = nc.vector.scalar_tensor_tensor(md[:, dst:dst + 8], md[:, mod:mod + 8], plus, par2[:, gain:gain + 8], ALU.add, ALU.mult)
                return ins

            def run2(is_ctx, l):
                at2, landed2, slot2 = at2_of(is_ctx, l)
                v = view2(is_ctx)
                n, B, tiles, per = v["L"], v["B"], v["tiles"], PC if is_ctx else PX
                link = Link(dve, sm2["link2_dve"], at2("link2_dve", 0)[1])

                dve.wait_ge(*at2("loaded2", 64))
                gains(0 if is_ctx else l, v["which"], link).then_inc(sm2["md_ready"], 1)
                dve.wait_ge(*at2("md_ready", 1))
                if not is_ctx:
                    nc.vector.tensor_copy(KALL[:, 0:LC], KCS[:, bass.ds(l * LC, LC)])
                    nc.vector.tensor_copy(VALL[:, 0:LC], VCS[:, bass.ds(l * LC, LC)])

                def pre_norm(r, g):
                    dve.wait_ge(*at2("rstd2", r + 1))
                    for c in range(KD):
                        nc.vector.scalar_tensor_tensor(v["XN"][c], v["X"][c], md[:, g + c:g + c + 1], v["RSTD"][0], ALU.mult, ALU.mult).then_inc(sm2["xs2"], 1)

                pre_norm(0, G1)

                def take(i, dst):
                    dve.wait_ge(*at2("acc2", i + 1))
                    nc.vector.tensor_copy(dst, ps[i % 2][:, 0:n]).then_inc(sm2[f"acc2_{i % 2}_free"], 1)

                def filter_arg(i):
                    h, kk = v["H12"], rot_t[0:64, 0:n]
                    b1, fr = (P_B1, P_FR1) if i == 0 else (P_B2, P_FR2)
                    rows = slice(0, 64)
                    dve.wait_ge(*at2("flt_in", i + 1))
                    link(nc.vector.tensor_scalar(h, ps[3][0:64, 0:n], p2c(b1, rows), p2c(fr, rows), ALU.add, ALU.mult))
                    link(nc.vector.tensor_scalar(kk, h, INV_2PI, None, ALU.mult))
                    link(nc.vector.tensor_scalar(kk, kk, MAGIC, None, ALU.add))
                    link(nc.vector.tensor_scalar(kk, kk, -MAGIC, None, ALU.add))
                    link(nc.vector.scalar_tensor_tensor(h, kk, -TP_A, h, ALU.mult, ALU.add))
                    link(nc.vector.scalar_tensor_tensor(h, kk, -TP_B, h, ALU.mult, ALU.add))
                    link(nc.vector.scalar_tensor_tensor(h, kk, -TP_C, h, ALU.mult, ALU.add))
                    nc.vector.tensor_scalar(h, h, PI, -PI, ALU.min, ALU.max).then_inc(sm2["flt_arg"], 1)

                def filter_decay():
                    for b in range(B):
                        dve.wait_ge(*at2("flt_h", b + 1))
                        nc.vector.tensor_tensor(v["HF"][b], ps[4 + b % 2][:], v["DEC"][b], ALU.mult).then_inc(sm2["flt_decayed"], 1)
                    dve.wait_ge(*at2("flt_decayed", B))
                    for b in range(B):
                        nc.vector.tensor_tensor(v["HP"][b], v["HF"][b][:, 0:256], v["HF"][b][:, 256:512], ALU.add)
                        ins = nc.vector.tensor_tensor(v["HM"][b], v["HF"][b][:, 0:256], v["HF"][b][:, 256:512], ALU.subtract)
                    ins.then_inc(sm2["flt_sums"], 1)

                def filter_inv():
                    dve.wait_ge(*at2("flt_norm", 1))
                    link(nc.vector.tensor_scalar(ninv[:], ps[3][:, 0:2], float(n), None, ALU.mult))
                    nc.vector.reciprocal(ninv[:], ninv[:]).then_inc(sm2["flt_inv"], 1)

                def head_norm(i):
                    dve.wait_ge(*at2("rstd2", 2 + i))
                    src = v["PX"][1 + i]
                    dst = v["KNEW"] if i == 0 else src
                    nc.vector.scalar_tensor_tensor(dst, src, p2c(P_GK if i == 0 else P_GQ), v["RSTD"][i % 2], ALU.mult, ALU.mult).then_inc(sm2["hn_normed"], 1)

                def head_turn(i):
                    dst = v["KNEW"] if i == 0 else v["PX"][1 + i]
                    dve.wait_ge(*at2("turn_ready", i + 1))
                    if i:
                        dve.wait_ge(*at2("hn_turned", i))
                    nc.vector.tensor_tensor(v["ROT"], ps[3][:, 0:n], v["SIN"], ALU.mult)
                    link(nc.vector.tensor_tensor(dst, dst, v["COS"], ALU.mult))
                    nc.vector.tensor_tensor(dst, dst, v["ROT"], ALU.add).then_inc(sm2["hn_turned"], 1)

                def values2():
                    for b in range(B):
                        dve.wait_ge(*at2("v2_ready", b + 1))
                        nc.vector.tensor_copy(v["V"][v["V0"] + b], ps[4 + b % 2][:, 0:P]).then_inc(sm2["v2_copied"], 1)

                def four_copy():
                    for b in range(B):
                        dve.wait_ge(*at2("four_ready", b + 1))
                        nc.vector.tensor_copy(v["FG"][b], ps[6 + b % 2][:]).then_inc(sm2["four_copied"], 1)

                def conv_sides(i, taps, which, dst):
                    dve.wait_ge(*at2("conv_mid", which + 1))
                    link(nc.vector.scalar_tensor_tensor(dst[:, 1:n], ps[i % 2][:, 0:n - 1], p2c(taps[0]), dst[:, 1:n], ALU.mult, ALU.add))
                    nc.vector.scalar_tensor_tensor(dst[:, 0:n - 1], ps[i % 2][:, 1:n], p2c(taps[1]), dst[:, 0:n - 1], ALU.mult, ALU.add).then_inc(sm2["conv2"], 1)
                    dve.wait_ge(*at2("conv2", which + 1))
                    dve.sem_inc(sm2[f"acc2_{i % 2}_free"], 1)

                between = {0: [lambda: filter_arg(0)], 1: [lambda: filter_arg(1)], 2: [filter_decay, lambda: head_norm(0)],
                           3: [filter_inv], 4: [lambda: head_turn(0), lambda: head_norm(1)],
                           5: [values2, lambda: head_norm(2)], 6: [lambda: head_turn(1), lambda: head_norm(3)],
                           7: [lambda: head_turn(2), lambda: head_norm(4)],
                           8: [lambda: head_turn(3)], 9: [lambda: head_turn(4)], 10: [four_copy]}
                for j in range(14):
                    if j in (1, 3, 5, 7):
                        take(j, v["PX"][j])
                    if j >= 8:
                        conv_sides(j, (P_HCW + j - 8, P_HCW + 12 + j - 8), j - 8, v["UC"][j - 8])
                    for step in between.get(j, []):
                        step()
                for i in range(2):
                    nc.vector.tensor_tensor(v["UC"][2 + i], v["UC"][2 + i], v["UC"][4 + i], ALU.mult).then_inc(sm2["u_ready"], 1)
                take(15, v["PX"][7])
                take(17, v["Y"][5])

                for i in range(len(tiles) + 4):
                    if i < len(tiles):
                        dve.wait_ge(*at2("sc2", i + 1))
                        o = 1536 + 1024 * (i % 2)
                        link(nc.vector.tensor_reduce(st_t[:, i:i + 1], ps_t[:, o:o + v["W"]], AX_X, ALU.max))
                        nc.vector.tensor_scalar(st_t[:, 32 + i:33 + i], st_t[:, i:i + 1], -0.125, None, ALU.mult).then_inc(sm2["neg2"], 1)
                    if 0 <= i - 1 < len(tiles):
                        t = i - 1
                        dve.wait_ge(*at2("pe2", t + 1))
                        link(nc.vector.reciprocal(st_t[:, 96 + t:97 + t], st_t[:, 64 + t:65 + t]))
                        pr = v["PR"][t % 2][:, 0:v["W"]]
                        nc.vector.tensor_scalar(pr, pr, st_t[:, 96 + t:97 + t], None, ALU.mult).then_inc(sm2["pn2"], 1)
                    if 0 <= i - 2 < len(tiles) and v["W"] > 512:
                        t = i - 2
                        dve.wait_ge(*at2("pt2", t + 1))
                        if t >= 2:
                            dve.wait_ge(*at2("o2", t - 1))
                        nc.vector.tensor_copy(v["PT"][t % 2][:, 512:v["W"]], ps[2][:, 0:v["W"] - 512]).then_inc(sm2["pd2"], 1)
                    if 0 <= i - 3 < len(tiles):
                        b, j, half = tiles[i - 3]
                        r = slice(64 * half, 64 * half + 64)
                        dve.wait_ge(*at2("o2", i - 2))
                        nc.vector.tensor_copy(v["Y"][j][r, b * P:(b + 1) * P], ps[0][r, 0:P]).then_inc(sm2["oc2"], 1)

                for b in range(B):
                    dve.wait_ge(*at2("ut_ready", b + 1))
                    nc.vector.tensor_copy(v["UT"][b], ps[3 + b % 2][:, 0:256]).then_inc(sm2["ut_copied"], 1)
                for f in range(B):
                    dve.wait_ge(*at2("us_ready", f + 1))
                    bank, sp = ps[5 + f % 2], v["SPEC"][f]
                    nc.vector.tensor_tensor(v["UM"][f], bank[:], sp, ALU.mult)
                    nc.vector.tensor_tensor(v["YR"][f], bank[:, 0:256], sp[:, 256:512], ALU.mult)
                    nc.vector.tensor_tensor(v["YI"][f], bank[:, 256:512], sp[:, 0:256], ALU.mult).then_inc(sm2["us_mul"], 1)
                for i in range(2):
                    y = v["Y"][6 + i]
                    dve.wait_ge(*at2("acc2", 19 + i))
                    link(nc.vector.tensor_scalar(y, v["UC"][2 + i], p2c(P_HB + i), None, ALU.mult))
                    nc.vector.scalar_tensor_tensor(y, ps[i][:, 0:n], ninv[:, i:i + 1], y, ALU.mult, ALU.add).then_inc(sm2[f"acc2_{i}_free"], 1)
                    dve.wait_ge(*at2(f"acc2_{i}_free", 10))
                    nc.vector.tensor_tensor(y, y, v["UC"][i], ALU.mult).then_inc(sm2["hy_out"], 1)

                def z_take(which, i0):
                    for c in range(KD):
                        i = i0 + c
                        dve.wait_ge(*at2("z2_squared", 8 * which + c + 1))
                        nc.vector.tensor_copy(v["XN"][c], ps[i % 2][:, 0:n]).then_inc(sm2[f"acc2_{i % 2}_free"], 1)

                def z_norm(which, r, i_end, g):
                    dve.wait_ge(*at2("rstd2", r + 1))
                    for b in range(2):
                        dve.wait_ge(*at2(f"acc2_{b}_free", i_end // 2))
                    for c in range(KD):
                        nc.vector.scalar_tensor_tensor(v["XN"][c], v["XN"][c], md[:, g + c:g + c + 1], v["RSTD"][0], ALU.mult, ALU.mult).then_inc(sm2["zn2"], 1)

                z_take(0, 20)
                z_norm(0, 6, 28, GA1)
                dve.wait_ge(*at2("x2_updated", 8))
                pre_norm(7, G2)
                with dve.Fori(0, FK // 2) as g:
                    for q in range(4):
                        i = 28 + q
                        dst = (v["AG"] if q % 2 == 0 else v["AV"])[q // 2]
                        c = g * 2 + q // 2 + FK * (q % 2)
                        sem, val = at2("conv_mid", 6 + q + 1)
                        dve.wait_ge(sem, g * 4 + val)
                        nc.vector.scalar_tensor_tensor(dst[:, 1:n], ps[i % 2][:, 0:n - 1], par2[:, bass.ds(P_FCW + c, 1)], dst[:, 1:n],
                                                       ALU.mult, ALU.add).then_inc(conv_left[0 if is_ctx else 1], 1)
                        dve.wait_ge(conv_left[0 if is_ctx else 1], g * 4 + (q + 1 if is_ctx else l * 2 * FK + q + 1))
                        nc.vector.scalar_tensor_tensor(dst[:, 0:n - 1], ps[i % 2][:, 1:n], par2[:, bass.ds(P_FCW + 4 * FK + c, 1)], dst[:, 0:n - 1],
                                                       ALU.mult, ALU.add).then_inc(sm2["conv2"], 1)
                        sem, val = at2("conv2", 6 + q + 1)
                        dve.wait_ge(sem, g * 4 + val)
                        dve.sem_inc(sm2[f"acc2_{i % 2}_free"], 1)
                z_take(1, 72)
                z_norm(1, 8, 80, GA2)
                if link.n != per["link2_dve"]:
                    raise AssertionError(f"link2_dve {is_ctx} {link.n}")

            run2(True, 0)
            v = view2(True)
            dve.wait_ge(sk["kv_loaded"], 16)
            link = Link(dve, kv_chain, 0)
            gains(1, 1, link).then_inc(sk["kv_md"], 1)
            dve.wait_ge(sk["kv_md"], 1)
            dve.wait_ge(sk["kv_rstd"], 1)
            for c in range(KD):
                nc.vector.scalar_tensor_tensor(v["XN"][c], v["X"][c], md[:, G1 + c:G1 + c + 1], v["RSTD"][0], ALU.mult, ALU.mult).then_inc(sk["kv_xs"], 1)
            dve.wait_ge(sk["kv_tr"], 1)
            nc.vector.tensor_copy(VCS[:, LC:2 * LC], ps[3][:, 0:LC]).then_inc(sk["kv_done"], 1)
            dve.wait_ge(sk["kv_krstd"], 1)
            nc.vector.scalar_tensor_tensor(KCS[:, LC:2 * LC], ps[1][:, 0:LC], p2c(P_GK), v["RSTD"][1], ALU.mult, ALU.mult).then_inc(sk["kv_done"], 1)
            dve.wait_ge(sk["kv_done"], 2)
            dve.sem_inc(sk["kv_done"], 1)
            with dve.Fori(0, DEPTH) as l:
                run2(False, l)

        @block.gpsimd
        def _(pool):
            pool.sem_inc(sm2["g_ready"], START2["g_ready"])
            with pool.Fori(0, DEPTH) as l:
                def at(name, i):
                    return sm[name], l * PER1[name] + i + START.get(name, 0)

                U = units()
                for u in range(len(U) + 1):
                    if u < len(U):
                        h, k = U[u]
                        pool.wait_ge(*at("sp_done", u + 1))
                        s = sp_t[:, (h % 2) * 1280 + OFF[k]:(h % 2) * 1280 + OFF[k] + P]
                        pool.sem_inc(waits_passed, 1)
                        pool.affine_select(out=s, in_=s, compare_op=ALU.is_gt, fill=0.0, base=0,
                                           pattern=[[1, P]], channel_multiplier=-1).then_inc(sm["sp_masked"], 1)
                    if u >= 1:
                        h, k = U[u - 1]
                        pool.wait_ge(*at("a_exp", u))
                        s = a_t[:, OFF[k]:OFF[k] + P]
                        pool.sem_inc(waits_passed, 1)
                        pool.affine_select(out=s, in_=s, compare_op=ALU.is_gt, fill=0.0, base=0,
                                           pattern=[[1, P]], channel_multiplier=-1).then_inc(sm["a_masked"], 1)
                for c in range(KD):
                    pool.wait_ge(*at("gate_sig", c + 1))
                    pool.tensor_tensor(H[GATE + c], H[GATE + c], H[c], ALU.mult).then_inc(sm["gate_mul"], 1)
                for c in range(KD):
                    pool.wait_ge(*at("zn_ready", c + 1))
                    pool.tensor_tensor(X[c], X[c], Z[c], ALU.add).then_inc(sm["x_updated"], 1)

            def run2(is_ctx, l):
                at2, landed2, slot2 = at2_of(is_ctx, l)
                v = view2(is_ctx)
                n, B = v["L"], v["B"]
                for f in range(B):
                    pool.wait_ge(*at2("us_mul", f + 1))
                    um = v["UM"][f]
                    pool.tensor_tensor(v["YI"][f], v["YI"][f], v["YR"][f], ALU.add).then_inc(pool_chain, 1)
                    pool.wait_ge(pool_chain, f + 1 if is_ctx else l * B + LC // P + f + 1)
                    pool.tensor_tensor(v["YR"][f], um[:, 0:256], um[:, 256:512], ALU.subtract).then_inc(sm2["us_done"], 1)

                def residual(which):
                    for c in range(KD):
                        pool.wait_ge(*at2("zn2", 8 * which + c + 1))
                        pool.tensor_tensor(v["X"][c], v["X"][c], v["XN"][c], ALU.add).then_inc(sm2["x2_updated"], 1)

                residual(0)
                with pool.Fori(0, FK // 2) as g:
                    for q in range(2):
                        sem, val = at2("gate_sig2", q + 1)
                        pool.wait_ge(sem, g * 2 + val)
                        pool.tensor_tensor(v["SG"][q], v["SG"][q], v["AG"][q], ALU.mult).then_inc(sm2["gate_mul2"], 1)
                        sem, val = at2("gate_mul2", q + 1)
                        pool.wait_ge(sem, g * 2 + val)
                        sem, val = at2("conv2", 6 + 2 * q + 2)
                        pool.wait_ge(sem, g * 4 + val)
                        pool.tensor_tensor(big[:, bass.ds((g * 2 + q) * n, n)], v["SG"][q], v["AV"][q], ALU.mult).then_inc(sm2["g_ready"], 1)
                residual(1)

            run2(True, 0)
            with pool.Fori(0, DEPTH) as l:
                run2(False, l)


def kernel(**inp):
    import numpy as np
    import concourse.bacc as bacc
    from concourse.bass_utils import run_bass_kernel_spmd as run

    f4 = np.float32

    def slots(w):
        k, m = w.shape
        return w.reshape(k // P, P, m // P, P).transpose(2, 1, 0, 3).reshape(m // P, P, k)

    def cols(v):
        return v.reshape(-1, P).T

    a = np.arange(P)
    c = np.zeros((P, C_END), f4)
    c[:, C_ONES:C_ONES + P] = 1.0
    c[:, C_BD:C_BD + P] = (a[:, None] // 64) == (a[None, :] // 64)
    c[:, C_ID:C_ID + P] = np.eye(P)
    c[:, C_NTRI:C_NTRI + P] = -1.0 * (a[:, None] >= a[None, :])
    c[:, C_NONE:C_NONE + P] = -1.0
    for i in range(16):
        c[64 + 16 + i, C_SWAP + i] = -1.0
        c[64 + i, C_SWAP + 16 + i] = 1.0
    c[:, C_CAUS:C_CAUS + P] = np.where(a[None, :] <= a[:, None], 0.0, -1e30)
    c[:, C_PREV:C_PREV + P] = np.where(a[None, :] > a[:, None], 0.0, -1e30)
    freq = (10000.0 ** (-np.arange(16, dtype=f4) / f4(16))).astype(f4)
    c[64:96, C_FREQ] = np.concatenate([freq, freq])
    for i in range(P):
        j = i % 32
        c[i + 16 if j < 16 else i - 16, C_SW2 + i] = -1.0 if j < 16 else 1.0

    w_in, w_out = inp["w_in"], inp["w_out"]
    head = lambda o, h, n=64: np.arange(o + h * n, o + (h + 1) * n)
    order = np.concatenate([head(0, 0), head(0, 2), head(0, 1), head(0, 3), np.arange(256, 512), np.arange(1280, 1664),
                            np.arange(1696, 2464), np.arange(512, 1280), np.arange(2464, 3488)])
    w1 = np.concatenate([np.concatenate([slots(w_in[l][:, order]), slots(w_out[l])]) for l in range(DEPTH)])
    mla_w = np.stack([np.concatenate([
        w_in[l][:, 1664:1696].reshape(KD, P, 32).transpose(1, 0, 2).reshape(P, 256),
        inp["mla_w_uq"][l].reshape(2, P, 384).transpose(1, 0, 2).reshape(P, 768),
        inp["mla_w_ukv"][l]], axis=1) for l in range(DEPTH)])
    p1 = np.stack([np.concatenate([
        cols(inp["norm_pre"][l]), cols(inp["norm_post"][l]), cols(inp["group_norm"][l]),
        inp["conv_w"][l].reshape(3, 2, P).transpose(2, 0, 1).reshape(P, 6), cols(inp["conv_b"][l]),
        cols(inp["mla_q_norm"][l]), cols(inp["mla_kv_norm"][l]),
        np.broadcast_to(inp["attn_sinks"][l], (P, 4))], axis=1) for l in range(DEPTH)])
    wmod = np.concatenate([slots(inp["w_mod_2"][l]) for l in range(DEPTH)])
    both = np.stack([cols(inp["c_2"][0]), cols(inp["c_ctx_2"])], axis=2).reshape(P, 16)
    modp = np.concatenate([np.repeat(cols(inp["b_mod_2"][l]), 2, axis=1) for l in range(DEPTH)] + [both], axis=1)
    w_in2, w_out2 = inp["w_in_2"], inp["w_out_2"]
    pairs = np.concatenate([np.concatenate([head(0, j), head(0, 4 + j)]) for j in range(4)])
    order2 = np.concatenate([np.arange(640, 768), np.arange(512, 640), pairs, np.arange(768, 1792)])
    rows2 = np.concatenate([pairs, np.arange(512, 1024)])
    up = np.concatenate([np.concatenate([np.arange(j * P, (j + 1) * P), np.arange((FK + j) * P, (FK + j + 1) * P)]) for j in range(FK)])
    w2 = np.concatenate([np.concatenate([
        slots(w_in2[l][:, order2]), slots(w_out2[l][rows2]), slots(inp["w_up_2"][l][:, up]),
        slots(inp["w_down_2"][l]).reshape(KD, P, FK, P).transpose(0, 2, 1, 3).reshape(FK, KD, P, P).transpose(0, 2, 1, 3).reshape(FK, P, D),
    ]) for l in range(DEPTH)])

    def rows(v, n=P):
        return np.concatenate([v, np.zeros((P - v.shape[0], v.shape[1]), v.dtype)]) if v.shape[0] < P else v

    def taps(w, chunks):
        return w.reshape(3, chunks, P).transpose(2, 0, 1).reshape(P, 3 * chunks)

    p2 = np.stack([np.concatenate([
        cols(inp["g_pre_mix_2"][l]), cols(inp["g_post_mix_2"][l]), cols(inp["g_pre_ffn_2"][l]), cols(inp["g_post_ffn_2"][l]),
        np.concatenate([inp["g_q_2"][l]] * 2).reshape(P, 1), np.concatenate([inp["g_k_2"][l]] * 2).reshape(P, 1),
        taps(inp["w_hy_conv_2"][l], 6), cols(inp["b_hy_conv_2"][l]),
        rows(inp["hy_b1_2"][l].reshape(64, 1)), rows(inp["hy_fr1_2"][l].reshape(64, 1)),
        rows(inp["hy_b2_2"][l].reshape(64, 1)), rows(inp["hy_fr2_2"][l].reshape(64, 1)),
        cols(inp["hy_bias_2"][l]), taps(inp["w_ffn_conv_2"][l], 2 * FK), cols(inp["b_ffn_conv_2"][l]),
        rows(inp["hy_w1_2"][l]), rows(inp["hy_w2_2"][l]), rows(inp["hy_w3_2"][l]),
        inp["w_fourier_2"][l].reshape(2, P, 256).transpose(1, 0, 2).reshape(P, 512)], axis=1) for l in range(DEPTH)])

    def tables_of(n):
        t = np.arange(n, dtype=np.float64)
        lay = lambda m: m.reshape(n // P, P, -1).transpose(1, 0, 2).reshape(P, -1)
        wide = np.zeros((8, P, max(n * n // P, 512 * n // P)), f4)
        put = lambda i, m: wide[i].__setitem__((slice(0, m.shape[0]), slice(0, m.shape[1])), m)
        a1 = 2 * np.pi / (2 * n) * np.outer(t, t + 0.5)
        a2 = 2 * np.pi / n * (np.outer(t, t) % n)
        a3 = 2 * np.pi / (2 * n) * np.outer(t + 0.5, t + 0.5)
        s2 = (64 * n) ** -0.5
        for i, m in enumerate((np.cos(a1), np.sin(a1), np.cos(a2) * s2, -np.sin(a2) * s2, np.cos(a3), np.sin(a3))):
            put(i, lay(m))
        lin = np.linspace(0.0, 1.0, n, dtype=f4)[:, None]
        bands = np.linspace(1e-4, 15, 16, dtype=f4)
        ang = (f4(2.0 * np.pi) * np.arange(n, dtype=f4)[:, None] / f4(n) * bands[None, :]).astype(f4)
        z = np.concatenate([lin, np.cos(ang), -np.sin(ang)], axis=-1)
        deltas = np.abs(np.linspace(np.log(1e-2) / 1.5, np.log(1e-2) / 0.3, 256, dtype=f4))
        decay = np.exp(-lin * deltas[None, :]).astype(f4)
        back = decay.copy()
        back[0] = 0.0
        put(6, lay(np.concatenate([decay, back], axis=1)))
        put(7, z.T)
        return wide

    fd = 2 * np.pi / 64 * (np.outer(np.arange(64), np.arange(64)) % 64)
    for i in range(2):
        c[64 * i:64 * i + 64, C_FD + 64 * i:C_FD + 64 * i + 64] = np.cos(fd)
        c[64 * i:64 * i + 64, C_FD + P + 64 * i:C_FD + P + 64 * i + 64] = np.sin(fd)
    inv = (10000.0 ** (-np.arange(0, 32, 2, dtype=f4) / 32)).astype(f4)
    ar = np.repeat(np.arange(8, dtype=f4), 64)[None, :] * inv[:, None]
    ac = np.tile(np.arange(64, dtype=f4), 8)[None, :] * inv[:, None]
    ang = np.concatenate([ar, ar, ac, ac] * 2)
    rope2 = np.stack([np.concatenate([np.cos(ang), np.ones((P, LC), f4)], axis=1),
                      np.concatenate([np.sin(ang), np.zeros((P, LC), f4)], axis=1)], axis=1)
    ctx_in = inp["ctx_2"][0].T.reshape(KD, P, LC)
    x_in = inp["x"][0].T.reshape(KD, P, T)
    arrays = dict(x_in=x_in, pos=np.broadcast_to(inp["positions"], (32, T)), w1=w1, mla_w=mla_w, p1=p1, consts=c,
                  wmod=wmod, modp=modp, ctx_in=ctx_in, w2=w2, p2=p2, tables=tables_of(T), tabs_c=tables_of(LC), rope2=rope2)
    nc = bacc.Bacc("TRN2", target_bir_lowering=False, num_devices=1)
    aps, maps = {}, {}
    for name, v in arrays.items():
        v = np.ascontiguousarray(v)
        maps[name + "_d"] = v
        aps[name] = nc.dram_tensor(name + "_d", v.shape, mybir.dt.from_np(v.dtype), kind="ExternalInput").ap()
    out = nc.dram_tensor("out_d", (KD, P, T), F32, kind="ExternalOutput").ap()
    build(nc, *(aps[n] for n in ("x_in", "ctx_in", "pos", "w1", "mla_w", "p1", "consts", "wmod", "modp", "w2", "p2",
                                 "tables", "tabs_c", "rope2")), out)
    r = run(nc, [maps], core_ids=[0])
    return r.results[0]["out_d"].reshape(D, T).T.reshape(1, T, D)
```
